# Optimizing a Trainium2 kernel written in Bass

```python
import jax, jax.numpy as jnp
from jax import lax
import numpy as np

D_MODEL = 1024
BATCH = 1
SEQ = 256
DEPTH = 2

D_MIX = D_MODEL
CONV_CH = D_MIX // 2
SGU_CH = D_MIX - CONV_CH
CONV_GROUPS = 8
SGU_HEADS = 4
SGU_HEAD_DIM = SGU_CH // SGU_HEADS
CONV_WIDTH = 31
CHUNK = 128
D_IN = 2 * CONV_CH + 2 * SGU_CH
D_FF = 2816
N_EXPERTS = 8
TOP_K = 2
N_DENSE = (DEPTH + 1) // 2
N_MOE = DEPTH // 2
EPS = 1e-6


def rms_norm(x, g):
    xf = x.astype(jnp.float32)
    y = xf * lax.rsqrt(jnp.mean(xf * xf, axis=-1, keepdims=True) + EPS)
    return (y * g.astype(jnp.float32)).astype(x.dtype)

def group_layer_norm(x, n_groups, g, b):
    shp = x.shape
    xf = x.astype(jnp.float32).reshape(shp[:-1] + (n_groups, shp[-1] // n_groups))
    mu = jnp.mean(xf, axis=-1, keepdims=True)
    var = jnp.mean(jnp.square(xf - mu), axis=-1, keepdims=True)
    y = ((xf - mu) * lax.rsqrt(var + EPS)).reshape(shp)
    return (y * g.astype(jnp.float32) + b.astype(jnp.float32)).astype(x.dtype)

def causal_depthwise_conv(c, w, b):
    y = lax.conv_general_dilated(
        c, w, window_strides=(1,), padding=[(CONV_WIDTH - 1, 0)],
        dimension_numbers=('NWC', 'WIO', 'NWC'), feature_group_count=c.shape[-1])
    return y + b

def hybrid_mixer(h, w_in, conv_w, conv_b, conv_ng, conv_nb, sgu_ng, sgu_nb, sgu_w, sgu_b, w_out):
    B, S, _ = h.shape
    z = jnp.einsum('bsd,de->bse', h, w_in)
    a, gate, u, v = jnp.split(z, [CONV_CH, 2 * CONV_CH, 2 * CONV_CH + SGU_CH], axis=-1)
    c = a * jax.nn.sigmoid(gate)
    c = causal_depthwise_conv(c, conv_w, conv_b)
    c = jax.nn.silu(group_layer_norm(c, CONV_GROUPS, conv_ng, conv_nb))
    u = jax.nn.gelu(u, approximate=False)
    v = group_layer_norm(jax.nn.gelu(v, approximate=False), SGU_HEADS, sgu_ng, sgu_nb)
    n_chunks = S // CHUNK
    vc = v.reshape(B, n_chunks, CHUNK, SGU_HEADS, SGU_HEAD_DIM)
    mask = jnp.tril(jnp.ones((CHUNK, CHUNK), dtype=bool))
    ws = jnp.where(mask[None], sgu_w, jnp.zeros((), sgu_w.dtype))
    sp = jnp.einsum('hts,bnshd->bnthd', ws, vc) + jnp.transpose(sgu_b)[None, None, :, :, None]
    g_out = u * sp.reshape(B, S, SGU_CH)
    y = jnp.concatenate([c, g_out], axis=-1)
    return jnp.einsum('bse,ed->bsd', y, w_out)

def swiglu(h, wg, wu, wd):
    return jnp.einsum('...f,fd->...d', jax.nn.silu(h @ wg) * (h @ wu), wd)

def moe_swiglu(h, router, wg, wu, wd):
    B, S, D = h.shape
    ht = h.reshape(B * S, D)
    logits = jnp.einsum('td,de->te', ht, router).astype(jnp.float32)
    top_vals, top_idx = lax.top_k(logits, TOP_K)
    gates = jax.nn.softmax(top_vals, axis=-1)
    dense_gate = jnp.sum(jax.nn.one_hot(top_idx, N_EXPERTS, dtype=jnp.float32) * gates[..., None], axis=1)
    dense_gate = dense_gate.astype(h.dtype)
    out = jnp.zeros_like(ht)
    for e in range(N_EXPERTS):
        out = out + dense_gate[:, e:e + 1] * swiglu(ht, wg[e], wu[e], wd[e])
    return out.reshape(B, S, D)

def first_inputs(seed: int = 0) -> dict:
    key = jax.random.key(seed)
    ks = jax.random.split(key, 24)
    nrm = lambda k, shp, s: jax.random.normal(k, shp, jnp.float32) * s
    L = DEPTH
    return {
        "x": nrm(ks[0], (BATCH, SEQ, D_MODEL), 1.0),
        "norm_mix": 1.0 + nrm(ks[1], (L, D_MODEL), 0.05),
        "w_in": nrm(ks[2], (L, D_MODEL, D_IN), D_MODEL ** -0.5),
        "conv_w": nrm(ks[3], (L, CONV_WIDTH, 1, CONV_CH), CONV_WIDTH ** -0.5),
        "conv_b": nrm(ks[4], (L, CONV_CH), 0.02),
        "conv_ng": 1.0 + nrm(ks[5], (L, CONV_CH), 0.05),
        "conv_nb": nrm(ks[6], (L, CONV_CH), 0.02),
        "sgu_ng": 1.0 + nrm(ks[7], (L, SGU_CH), 0.05),
        "sgu_nb": nrm(ks[8], (L, SGU_CH), 0.02),
        "sgu_w": nrm(ks[9], (L, SGU_HEADS, CHUNK, CHUNK), CHUNK ** -0.5),
        "sgu_b": 1.0 + nrm(ks[10], (L, SGU_HEADS, CHUNK), 0.1),
        "w_out": nrm(ks[11], (L, D_MIX, D_MODEL), D_MIX ** -0.5),
        "norm_ffn": 1.0 + nrm(ks[12], (L, D_MODEL), 0.05),
        "ffn_wg": nrm(ks[13], (N_DENSE, D_MODEL, D_FF), D_MODEL ** -0.5),
        "ffn_wu": nrm(ks[14], (N_DENSE, D_MODEL, D_FF), D_MODEL ** -0.5),
        "ffn_wd": nrm(ks[15], (N_DENSE, D_FF, D_MODEL), D_FF ** -0.5),
        "moe_router": nrm(ks[16], (N_MOE, D_MODEL, N_EXPERTS), D_MODEL ** -0.5),
        "moe_wg": nrm(ks[17], (N_MOE, N_EXPERTS, D_MODEL, D_FF), D_MODEL ** -0.5),
        "moe_wu": nrm(ks[18], (N_MOE, N_EXPERTS, D_MODEL, D_FF), D_MODEL ** -0.5),
        "moe_wd": nrm(ks[19], (N_MOE, N_EXPERTS, D_FF, D_MODEL), D_FF ** -0.5),
        "norm_final": 1.0 + nrm(ks[20], (D_MODEL,), 0.05),
    }

def first_block(x, norm_mix, w_in, conv_w, conv_b, conv_ng, conv_nb, sgu_ng, sgu_nb, sgu_w, sgu_b,
              w_out, norm_ffn, ffn_wg, ffn_wu, ffn_wd, moe_router, moe_wg, moe_wu, moe_wd, norm_final):
    for l in range(DEPTH):
        h = rms_norm(x, norm_mix[l])
        x = x + hybrid_mixer(h, w_in[l], conv_w[l], conv_b[l], conv_ng[l], conv_nb[l],
                             sgu_ng[l], sgu_nb[l], sgu_w[l], sgu_b[l], w_out[l])
        h = rms_norm(x, norm_ffn[l])
        i = l // 2
        if l % 2 == 0:
            x = x + swiglu(h, ffn_wg[i], ffn_wu[i], ffn_wd[i])
        else:
            x = x + moe_swiglu(h, moe_router[i], moe_wg[i], moe_wu[i], moe_wd[i])
    return rms_norm(x, norm_final)


DEPTH_2 = 1

N_ATT_HEADS = 8
HEAD_DIM = 64
ATT_WIDTH = N_ATT_HEADS * HEAD_DIM
Q_BLOCK = 128
CONV_WIDTH_2 = 512
CONV_K = 3
N_GROUPS = 4
EXPERTS_PER_GROUP = 4
N_EXPERTS_2 = N_GROUPS * EXPERTS_PER_GROUP
TOP_K_IN_GROUP = 2
D_EXPERT = 256
PLE_DIM = 256
NEG_INF = -1e30

PROJ_SIZES = (ATT_WIDTH, ATT_WIDTH, ATT_WIDTH, N_ATT_HEADS,
              CONV_WIDTH_2, CONV_WIDTH_2, CONV_WIDTH_2, D_MODEL, D_MODEL)
PROJ_WIDTH = 3 * ATT_WIDTH + N_ATT_HEADS + 3 * CONV_WIDTH_2 + 2 * D_MODEL


def rms_norm_2(x, g):
    xf = x.astype(jnp.float32)
    y = xf * lax.rsqrt(jnp.mean(xf * xf, axis=-1, keepdims=True) + EPS)
    return (y * g.astype(jnp.float32)).astype(x.dtype)

def split_offsets():
    offs, acc = [], 0
    for s in PROJ_SIZES[:-1]:
        acc += s
        offs.append(acc)
    return offs

def forgetting_attention(q, k, v, log_f):
    b, s, h, d = q.shape
    n_blocks = s // Q_BLOCK
    c = jnp.cumsum(log_f, axis=1).transpose(0, 2, 1)
    qh = q.transpose(0, 2, 1, 3)
    kh = k.transpose(0, 2, 1, 3)
    vh = v.transpose(0, 2, 1, 3)
    q_blocks = jnp.moveaxis(qh.reshape(b, h, n_blocks, Q_BLOCK, d), 2, 0)
    c_blocks = jnp.moveaxis(c.reshape(b, h, n_blocks, Q_BLOCK), 2, 0)
    key_pos = jnp.arange(s)
    scale = HEAD_DIM ** -0.5

    def one_block(args):
        qb, cqb, blk = args
        q_pos = blk * Q_BLOCK + jnp.arange(Q_BLOCK)
        logits = jnp.einsum('bhqd,bhkd->bhqk', qb, kh).astype(jnp.float32) * scale
        logits = logits + (cqb[..., :, None] - c[..., None, :])
        causal = key_pos[None, :] <= q_pos[:, None]
        logits = jnp.where(causal, logits, NEG_INF)
        probs = jax.nn.softmax(logits, axis=-1)
        return jnp.einsum('bhqk,bhkd->bhqd', probs.astype(vh.dtype), vh)

    out = lax.map(one_block, (q_blocks, c_blocks, jnp.arange(n_blocks)))
    out = out.transpose(1, 0, 3, 2, 4).reshape(b, s, h * d)
    return out

def causal_short_conv(u, w):
    s = u.shape[1]
    u_pad = jnp.pad(u, ((0, 0), (CONV_K - 1, 0), (0, 0)))
    y = w[0] * u_pad[:, 0:s]
    for j in range(1, CONV_K):
        y = y + w[j] * u_pad[:, j:j + s]
    return y

def hierarchical_moe(h, w_rg, b_rg, w_re, b_re, w_gate, w_up, w_down):
    b, s, d = h.shape
    ht = h.reshape(b * s, d)
    g_logits = (ht @ w_rg + b_rg).astype(jnp.float32)
    g_prob = jax.nn.softmax(g_logits, axis=-1)
    g_val, g_idx = lax.top_k(g_prob, 1)
    e_logits = (ht @ w_re + b_re).astype(jnp.float32)
    e_logits = e_logits.reshape(-1, N_GROUPS, EXPERTS_PER_GROUP)
    e_in = jnp.take_along_axis(e_logits, g_idx[:, :, None], axis=1)[:, 0]
    e_prob = jax.nn.softmax(e_in, axis=-1)
    e_val, e_idx = lax.top_k(e_prob, TOP_K_IN_GROUP)
    e_val = e_val / jnp.sum(e_val, axis=-1, keepdims=True)
    gate = g_val * e_val
    global_idx = g_idx * EXPERTS_PER_GROUP + e_idx
    combine = jnp.sum(jax.nn.one_hot(global_idx, N_EXPERTS_2, dtype=jnp.float32)
                      * gate[..., None], axis=1)
    a = jnp.einsum('td,edf->tef', ht, w_gate)
    u = jnp.einsum('td,edf->tef', ht, w_up)
    hid = jax.nn.silu(a) * u * combine[..., None].astype(ht.dtype)
    out = jnp.einsum('tef,efd->td', hid, w_down)
    return out.reshape(b, s, d)

def second_inputs(seed: int = 0) -> dict:
    key = jax.random.key(seed)
    ks = jax.random.split(key, 24)
    L, D = DEPTH_2, D_MODEL
    f32 = jnp.float32

    def nrm(k, shape, scale):
        return jax.random.normal(k, shape, f32) * scale

    def gain(k, shape):
        return 1.0 + 0.05 * jax.random.normal(k, shape, f32)

    return {
        "x": nrm(ks[0], (BATCH, SEQ, D), 1.0),
        "p": nrm(ks[1], (DEPTH_2, BATCH, SEQ, PLE_DIM), 1.0),
        "attn_norm_g": gain(ks[2], (L, D)),
        "w_in": nrm(ks[3], (L, D, PROJ_WIDTH), D ** -0.5),
        "b_f": 1.0 + 3.0 * jax.random.uniform(ks[4], (L, N_ATT_HEADS), f32),
        "q_norm_g": gain(ks[5], (L, HEAD_DIM)),
        "k_norm_g": gain(ks[6], (L, HEAD_DIM)),
        "conv_w": nrm(ks[7], (L, CONV_K, CONV_WIDTH_2), CONV_K ** -0.5),
        "w_out_att": nrm(ks[8], (L, ATT_WIDTH, D), ATT_WIDTH ** -0.5),
        "w_out_conv": nrm(ks[9], (L, CONV_WIDTH_2, D), CONV_WIDTH_2 ** -0.5),
        "w_o": nrm(ks[10], (L, D, D), D ** -0.5),
        "ffn_norm_g": gain(ks[11], (L, D)),
        "w_rg": nrm(ks[12], (L, D, N_GROUPS), D ** -0.5),
        "b_rg": nrm(ks[13], (L, N_GROUPS), 0.01),
        "w_re": nrm(ks[14], (L, D, N_EXPERTS_2), D ** -0.5),
        "b_re": nrm(ks[15], (L, N_EXPERTS_2), 0.01),
        "w_gate": nrm(ks[16], (L, N_EXPERTS_2, D, D_EXPERT), D ** -0.5),
        "w_up": nrm(ks[17], (L, N_EXPERTS_2, D, D_EXPERT), D ** -0.5),
        "w_down": nrm(ks[18], (L, N_EXPERTS_2, D_EXPERT, D), D_EXPERT ** -0.5),
        "ple_norm_g": gain(ks[19], (L, D)),
        "w_pg": nrm(ks[20], (L, D, D), D ** -0.5),
        "w_ple": nrm(ks[21], (L, PLE_DIM, D), PLE_DIM ** -0.5),
    }

def second_block(x, p, attn_norm_g, w_in, b_f, q_norm_g, k_norm_g, conv_w, w_out_att,
              w_out_conv, w_o, ffn_norm_g, w_rg, b_rg, w_re, b_re, w_gate, w_up, w_down,
              ple_norm_g, w_pg, w_ple):
    b, s, _ = x.shape
    offs = split_offsets()
    for i in range(DEPTH_2):
        h = rms_norm_2(x, attn_norm_g[i])
        proj = h @ w_in[i]
        q, k, v, f_logit, cb, cc, cu, ga, gb = jnp.split(proj, offs, axis=-1)

        q = rms_norm_2(q.reshape(b, s, N_ATT_HEADS, HEAD_DIM), q_norm_g[i])
        k = rms_norm_2(k.reshape(b, s, N_ATT_HEADS, HEAD_DIM), k_norm_g[i])
        v = v.reshape(b, s, N_ATT_HEADS, HEAD_DIM)
        log_f = jax.nn.log_sigmoid(f_logit.astype(jnp.float32) + b_f[i].astype(jnp.float32))
        y_att = forgetting_attention(q, k, v, log_f)

        y_conv = cb * causal_short_conv(cc * cu, conv_w[i])

        merged = (jax.nn.sigmoid(ga) * (y_att @ w_out_att[i])
                  + jax.nn.sigmoid(gb) * (y_conv @ w_out_conv[i]))
        x = x + merged @ w_o[i]

        h2 = rms_norm_2(x, ffn_norm_g[i])
        x = x + hierarchical_moe(h2, w_rg[i], b_rg[i], w_re[i], b_re[i],
                                 w_gate[i], w_up[i], w_down[i])

        h3 = rms_norm_2(x, ple_norm_g[i])
        x = x + jax.nn.sigmoid(h3 @ w_pg[i]) * (p[i] @ w_ple[i])
    return x


def setup_inputs(seed=0):
    out = dict(first_inputs(seed))
    for name, value in second_inputs(seed + 1).items():
        if name != "x":
            out[name + "_2"] = value
    return out


def reference(
    x, norm_mix, w_in, conv_w, conv_b, conv_ng, conv_nb, sgu_ng, sgu_nb, sgu_w, sgu_b, w_out,
    norm_ffn, ffn_wg, ffn_wu, ffn_wd, moe_router, moe_wg, moe_wu, moe_wd, norm_final, p_2,
    attn_norm_g_2, w_in_2, b_f_2, q_norm_g_2, k_norm_g_2, conv_w_2, w_out_att_2, w_out_conv_2,
    w_o_2, ffn_norm_g_2, w_rg_2, b_rg_2, w_re_2, b_re_2, w_gate_2, w_up_2, w_down_2,
    ple_norm_g_2, w_pg_2, w_ple_2,
):
    x = first_block(
        x, norm_mix, w_in, conv_w, conv_b, conv_ng, conv_nb, sgu_ng, sgu_nb, sgu_w, sgu_b,
        w_out, norm_ffn, ffn_wg, ffn_wu, ffn_wd, moe_router, moe_wg, moe_wu, moe_wd, norm_final,
    )
    return second_block(
        x, p_2, attn_norm_g_2, w_in_2, b_f_2, q_norm_g_2, k_norm_g_2, conv_w_2, w_out_att_2,
        w_out_conv_2, w_o_2, ffn_norm_g_2, w_rg_2, b_rg_2, w_re_2, b_re_2, w_gate_2, w_up_2,
        w_down_2, ple_norm_g_2, w_pg_2, w_ple_2,
    )


_drawn_inputs = setup_inputs


def setup_inputs(seed=0):
    import zlib

    import numpy as np

    out = dict(_drawn_inputs(seed))
    spreads = {}
    factors = {'conv_nb': 2.912,
     'sgu_nb': 3.105,
     'q_norm_g_2': 3.157,
     'k_norm_g_2': 4.752,
     'b_rg_2': 6.428,
     'b_re_2': 8.0,
     'ple_norm_g_2': 6.398}
    for name, (base, spread) in spreads.items():
        noise = np.random.default_rng([zlib.crc32(name.encode()), seed]).standard_normal(out[name].shape)
        drawn = base * np.exp(spread * noise) if base else spread * noise
        out[name] = __import__('jax').numpy.asarray(drawn.astype(out[name].dtype))
    for name, factor in factors.items():
        out[name] = (out[name] * factor).astype(out[name].dtype)
    return out
```

```python
from contextlib import ExitStack, contextmanager

import concourse.bass as bass
from concourse import mybir

F32 = mybir.dt.float32
I32 = mybir.dt.int32
ALU = mybir.AluOpType
ACT = mybir.ActivationFunctionType
AX_X = mybir.AxisListType.X

P = 128
S = 256
TT = S // P
D = 1024
KC = D // P
EPS = 1e-6
HALF = 512
CH = 4
TAPS = 31
PAD = TAPS - 1
D_FF = 2816
FFC = D_FF // P
GROUPS = 6
EXPERTS = 8
HEADS = 8
TAPS2 = 3
DE = 256
GROUPS2 = 4
CAP = 96
PASSES = -(-S // CAP)
SLOTS = 6
TILE = 4096
NEG = -1.0e30

INS = ["x", "norm_mix", "w_in", "conv_w", "conv_b", "conv_ng", "conv_nb", "sgu_ng", "sgu_nb", "sgu_w",
       "sgu_b", "w_out", "norm_ffn", "ffn_wg", "ffn_wu", "ffn_wd", "moe_router", "moe_wg", "moe_wu",
       "moe_wd", "norm_final", "p_2", "attn_norm_g_2", "w_in_2", "b_f_2", "q_norm_g_2", "k_norm_g_2",
       "conv_w_2", "w_out_att_2", "w_out_conv_2", "w_o_2", "ffn_norm_g_2", "w_rg_2", "b_rg_2", "w_re_2",
       "b_re_2", "w_gate_2", "w_up_2", "w_down_2", "ple_norm_g_2", "w_pg_2", "w_ple_2"]


class Own:

    def __init__(self, eng, sem):
        self.eng, self.sem, self.n, self.turns = eng, sem, 0, 0

    def mark(self, ins):
        ins.then_inc(self.sem, 1)
        self.n += 1

    def settle(self, behind=0):
        self.eng.wait_ge(self.sem, self.turns + (self.n - behind))

    def link(self, ins):
        self.mark(ins)
        self.settle()

    @contextmanager
    def loop(self, i, trips, per):
        start, self.turns = self.n, i * per
        yield
        assert self.n - start == per, (self.n - start, per)
        self.n, self.turns = start + per * trips, 0


class Freed:

    def __init__(self, sem, at, each=0):
        self.sem, self.at, self.each = sem, at, each

    def wait(self, eng, i=None):
        eng.wait_ge(self.sem, self.at if i is None else i * self.each + self.at)


class Stream:

    def __init__(self, landed, first_slot=0):
        self.landed, self.total = landed, [0] * SLOTS
        self.t, self.where, self.segments = first_slot, {}, []

    def segment(self, tiles, trips=1):
        per, t0 = [0] * SLOTS, self.t
        for j, (_, n, _, _) in enumerate(tiles):
            per[(t0 + j) % SLOTS] += 16 * n
        inside = [0] * SLOTS
        for j, (name, n, _, _) in enumerate(tiles):
            s = (t0 + j) % SLOTS
            inside[s] += 16 * n
            self.where[name] = (s, self.total[s] + inside[s], per[s])
        assert trips == 1 or len(tiles) % SLOTS == 0
        for s in range(SLOTS):
            self.total[s] += per[s] * trips
        self.t += len(tiles) * trips
        self.segments.append((t0, tiles, trips))

    def arrived(self, eng, name, i=None):
        s, at, each = self.where[name]
        eng.wait_ge(self.landed[s], at if i is None else i * each + at)
        return s


def build(nc, A, out):
    ctx = ExitStack()
    with ctx:
        def sb(name, shape, dt=F32):
            return ctx.enter_context(nc.sbuf_tensor(name, shape, dt))

        def sem(name):
            return ctx.enter_context(nc.semaphore(name))

        ring = sb("ring", [P, SLOTS, TILE])
        x = sb("x_res", [P, TT, D])
        h = sb("h", [P, TT, D])
        hT = sb("hT", [P, KC, S])
        yT = sb("yT", [P, KC, S])
        gain = sb("gain", [P, 2, D])
        work = sb("work", [P, 5, D])
        wk = [work[:, i, :] for i in range(5)]
        cpad = sb("cpad", [P, CH, PAD + S])
        uT = sb("uT", [P, CH, S])
        vn = sb("vn", [P, TT, HALF])
        xg = sb("xg", [P, KC, CAP])
        pick = sb("pick", [P, TT, CAP])
        pickg = sb("pickg", [P, TT, CAP])
        spread = sb("spread", [P, S])
        ident = sb("ident", [P, P])
        upper = sb("upper", [P, P])
        above = sb("above", [P, P])
        ones = sb("ones", [P, P])
        block64 = sb("block64", [P, P])
        causal = sb("causal", [P, S])
        tie = sb("tie", [P, EXPERTS, EXPERTS])
        head_row = sb("head_row", [P, HEADS, P])
        slot_i = sb("slot_i", [P, CAP], I32)
        slot_no = sb("slot_no", [P, CAP])
        sgu = sb("sgu", [P, 4, D])
        wsT = sgu[:, 0, :].rearrange("p (l h t) -> p l h t", l=2, h=4)
        sgb = sgu[:, 1, :].rearrange("p (l h t) -> p l h t", l=2, h=4)
        sng = sgu[:, 2, :].rearrange("p (l n) -> p l n", l=2)
        snb = sgu[:, 3, :].rearrange("p (l n) -> p l n", l=2)
        qz = h[:].rearrange("p t (a s) -> p (t a) s", s=S)
        L1 = hT[:]
        L0 = work[:, 4, :].rearrange("p (h k) -> p h k", h=HEADS)
        PT = work[:, 0:2, :].rearrange("p a (b s) -> p (a b) s", s=P)
        NROW = 38
        rows = work[0:NROW, 2, 0:P]
        rowsw = work[0:CH * TAPS, 2, P:3 * P].rearrange("p (l n) -> p l n", l=2)
        pcol = sb("pcol", [P, NROW])
        wcol = sb("wcol", [P, 2, CH * TAPS])
        router1 = sb("router1", [P, KC, EXPERTS])
        router2 = sb("router2", [P, KC, 20])
        wf = sb("wf", [P, KC, HEADS])
        bias2 = sb("bias2", [P, 20])
        bf = sb("bf", [P, HEADS])
        eps_c = sb("eps_c", [P, 1])
        half_c = sb("half_c", [P, 8])
        ms = sb("ms", [P, 8])
        rstd = sb("rstd", [P, 8])
        ss = sb("ss", [P, 2])
        s8 = sb("s8", [P, 8])
        lg = sb("lg", [P, TT, 20])
        shifted = sb("shifted", [P, TT, 20])
        ex = sb("ex", [P, TT, 20])
        mk = sb("mk", [P, TT, 20])
        cnt = sb("cnt", [P, TT, 20])
        mx = sb("mx", [P, 2 + 8])
        den = sb("den", [P, 2 + 8])
        pair_gt, pair_eq = (work[:, 3, k * P:(k + 1) * P] for k in range(2))
        ntab = (PASSES * EXPERTS) + 1
        table = sb("table", [P, ntab, 3, TT])
        table2 = sb("table2", [P, PASSES * GROUPS2 + 1, 6, TT])
        now = sb("now", [P, 3, TT])
        now2 = sb("now2", [P, 6, TT])
        cws = sb("cws", [P, 4])
        over_f = sb("over_f", [P, 2])
        over = sb("over", [1, 2], I32)
        ptok = work[:, 3, 0:TT * DE].rearrange("p (t d) -> p t d", t=TT)
        negmax = sb("negmax", [P, TT, HEADS])
        rowsum = sb("rowsum", [P, TT, HEADS])
        pT = sb("pT", [P, 2, S])
        c8 = sb("c8", [P, TT, HEADS])
        negc = sb("negc", [P, S])
        lf = sb("lf", [P, TT, HEADS])
        hs = sb("hs", [P, 6, HEADS])
        tick = sb("tick", [1, 4])
        PS = ctx.enter_context(nc.psum_tensor("PS", [P, 8, HALF], F32))

        def bank(b, n=1):
            return PS[:, b:b + n, :].rearrange("p b n -> p (b n)")

        def chunks(b, n=2):
            return PS[:, b:b + n, :].rearrange("p b (c s) -> p (b c) s", s=S)

        x_landed = sem("x_landed")
        sgu_landed = sem("sgu_landed")
        rows_landed = sem("rows_landed")
        small_landed = sem("small_landed")
        gain_landed = [sem(f"gain_landed{i}") for i in range(2)]
        consts_made = sem("consts_made")
        consts_step = sem("consts_step")
        sgu_masked = sem("sgu_masked")
        params_turned = sem("params_turned")
        params_ready = sem("params_ready")
        landed = [sem(f"landed{s}") for s in range(SLOTS)]
        vstep = sem("vector_step")
        x_updated = sem("x_updated")
        sumsq_ready, ms_ready, rstd_ready = sem("sumsq_ready"), sem("ms_ready"), sem("rstd_ready")
        norm_applied, h_turned = sem("norm_applied"), sem("h_turned")
        hT_by_scalar, hT_by_vector = sem("hT_by_scalar"), sem("hT_by_vector")
        proj_done, gate_act, v_act, u_act = sem("proj_done"), sem("gate_act"), sem("v_act"), sem("u_act")
        conv_done, mean_done, centred, squared = sem("conv_done"), sem("mean_done"), sem("centred"), sem("squared")
        var_done, std_done, conv_hat, conv_act = sem("var_done"), sem("std_done"), sem("conv_hat"), sem("conv_act")
        v_centred, v_squared, v_ready = sem("v_centred"), sem("v_squared"), sem("v_ready")
        mixed, sgu_out, out_done = sem("mixed"), sem("sgu_out"), sem("out_done")
        gu_ready, silu_ready, hid_ready, down_done = (sem("ffn_gu_ready"), sem("ffn_silu_ready"),
                                                      sem("ffn_hid_ready"), sem("ffn_down_done"))
        logits_ready, mask_ready, rank_ready = sem("logits_ready"), sem("mask_ready"), sem("rank_ready")
        exps_wanted, exps_ready = sem("exps_wanted"), sem("exps_ready")
        over_ready = sem("over_ready")

        class Pass:

            def __init__(self, name):
                self.picked = sem(f"{name}_picked")
                self.gathered = sem(f"{name}_gathered")
                self.xg_by_scalar = sem(f"{name}_xg_by_scalar")
                self.xg_by_vector = sem(f"{name}_xg_by_vector")
                self.gu_ready = sem(f"{name}_gu_ready")
                self.silu_ready = sem(f"{name}_silu_ready")
                self.hid_ready = sem(f"{name}_hid_ready")
                self.down_done = sem(f"{name}_down_done")
                self.y_by_scalar = sem(f"{name}_y_by_scalar")
                self.y_by_vector = sem(f"{name}_y_by_vector")
                self.scattered = sem(f"{name}_scattered")
                self.added = sem(f"{name}_added")
                self.vstep = sem(f"{name}_vector_step")

        main1, rest1 = Pass("moe"), Pass("moe_rest")
        main2, rest2 = Pass("moe2"), Pass("moe2_rest")
        rest_landed = [[sem(f"rest{k}_landed{s}") for s in range(SLOTS)] for k in (1, 2)]

        proj2 = sem("proj2_done")
        f_ready, log_step, cum_ready, cum_copied = (
            sem(n) for n in ("f_ready", "log_step", "cum_ready", "cum_copied"))
        ABS_Z, EXP_Z, LN_Z, LOG_F = 1, 2, 3, 4
        qk_sq, qk_ms, qk_std, qk_hat = sem("qk_squared"), sem("qk_meansq"), sem("qk_std"), sem("qk_hat")
        v2_copied, cbu_copied, cc_used, yconv = (
            sem(n) for n in ("v2_copied", "cb_cu_copied", "cc_used", "yconv_ready"))
        gates_act = sem("gates_act")
        att_logits, att_shift, att_max, att_exp, att_turned, att_pT_s, att_pT_v, att_out, att_y, att_yturned, att_yT = (
            sem(n) for n in ("att_logits", "att_shifted", "att_max", "att_exp", "att_turned", "att_pT_scalar", "att_pT_vector",
                             "att_out", "att_y", "att_yturned", "att_yT"))
        merge_mm, merged, o_done = sem("merge_mm"), sem("merged"), sem("o_done")
        pw_done, pg_done, pg_act = (sem(n) for n in ("pw_done", "pg_done", "pg_act"))
        stored = sem("stored")

        def slot(s):
            return ring[:, s, :]

        def by8(s):
            return ring[:, s, :].rearrange("p (k n) -> p k n", k=KC)

        def by4(s):
            return ring[:, s, :].rearrange("p (k n) -> p k n", k=4)

        def cols(w, c0, n):
            return w[:, c0:c0 + n].rearrange("(k p) n -> p k n", p=P)

        def kays(w, k0, n):
            return w[k0 * P:(k0 + n) * P, :].rearrange("(k p) n -> p k n", p=P)

        def expert(w, i):
            if isinstance(i, int):
                return w[i]
            return w[bass.ds(i, 1), :, :].rearrange("a r c -> (a r) c")

        stream = Stream(landed)

        def fixed(name, s_view, src, freed):
            return (name, 1, lambda i, s: [(s_view(s), src)], freed)

        def mixer_tiles(l):
            w, wo = A["w_in"][l], A["w_out"][l]
            return [fixed((l, "gate"), by8, cols(w, 512, 512), Freed(proj_done, 4 * l + 1)),
                    fixed((l, "a"), by8, cols(w, 0, 512), Freed(proj_done, 4 * l + 2)),
                    fixed((l, "v"), by8, cols(w, 1536, 512), Freed(proj_done, 4 * l + 3)),
                    fixed((l, "u"), by8, cols(w, 1024, 512), Freed(proj_done, 4 * l + 4)),
                    fixed((l, "out_sgu"), by4, kays(wo, 4, 4), Freed(out_done, 4 * l + 2)),
                    fixed((l, "out_conv"), by4, kays(wo, 0, 4), Freed(out_done, 4 * l + 4))]

        def ffn_chunks(j):
            return min(4, FFC - 4 * j)

        def ffn_tiles(key, wg, wu, wd, freed_gu, freed_d):
            def gu(kind, w, j):
                n = P * ffn_chunks(j)
                return ((key, kind, j), 1,
                        lambda i, s: [(by8(s)[:, :, 0:n], cols(w(i), 4 * P * j, n))], freed_gu(j))

            def dn(j):
                n = ffn_chunks(j)
                return ((key, "d", j), 1, lambda i, s: [(by4(s)[:, 0:n, :], kays(wd(i), 4 * j, n))], freed_d(j))

            tiles = []
            for j in range(GROUPS):
                tiles += [gu("g", wg, j), gu("u", wu, j)]
                if j:
                    tiles.append(dn(j - 1))
            return tiles + [dn(GROUPS - 1)]

        def moe_tiles(s, key, each=GROUPS):
            return ffn_tiles(key, lambda i: expert(A["moe_wg"][0], i), lambda i: expert(A["moe_wu"][0], i),
                             lambda i: expert(A["moe_wd"][0], i),
                             lambda j: Freed(s.gu_ready, j + 1, each), lambda j: Freed(s.down_done, j + 1, each))

        def w2_gu(g, q, s):
            v = slot(s).rearrange("p (w k n) -> p w k n", w=2, k=KC)
            return [(v[:, w], expert(A[n][0], g * 4 + q).rearrange("(k p) n -> p k n", p=P))
                    for w, n in enumerate(("w_gate_2", "w_up_2"))]

        def w2_d(g, q, s):
            v = slot(s).rearrange("p (e k n) -> p e k n", e=2, k=2)
            return [(v[:, e], expert(A["w_down_2"][0], g * 4 + q + e).rearrange("(k p) n -> p k n", p=P))
                    for e in range(2)]

        def moe2_tiles(s, key):
            gu = [((key, "gu", q), 2, (lambda q: lambda i, s_: w2_gu(i, q, s_))(q), Freed(s.gu_ready, q + 1, 4))
                  for q in range(4)]
            dn = [((key, "d", q), 2, (lambda q: lambda i, s_: w2_d(i, q, s_))(q), Freed(s.down_done, q + 2, 4))
                  for q in (0, 2)]
            return [gu[0], gu[1], gu[2], dn[0], gu[3], dn[1]]

        stream.segment(mixer_tiles(0))
        stream.segment(ffn_tiles("ffn", lambda i: A["ffn_wg"][0], lambda i: A["ffn_wu"][0], lambda i: A["ffn_wd"][0],
                                 lambda j: Freed(gu_ready, min(2 * j + 2, 11)),
                                 lambda j: Freed(down_done, min(2 * j + 2, 11))))
        stream.segment(mixer_tiles(1))
        stream.segment(moe_tiles(main1, "moe"), EXPERTS)
        w2 = A["w_in_2"][0]
        two = [("q", 0), ("k", 512), ("v", 1024), ("cb", 1544), ("cc", 2056), ("cu", 2568),
               ("ga0", 3080), ("ga1", 3592), ("gb0", 4104), ("gb1", 4616)]
        stream.segment([fixed(n, by8, cols(w2, c, 512), Freed(proj2, k + 1)) for k, (n, c) in enumerate(two)]
                       + [fixed("out_att", by4, kays(A["w_out_att_2"][0], 0, 4), Freed(merge_mm, 2)),
                          fixed("out_conv2", by4, kays(A["w_out_conv_2"][0], 0, 4), Freed(merge_mm, 4)),
                          fixed("o0", by4, kays(A["w_o_2"][0], 0, 4), Freed(o_done, 2)),
                          fixed("o1", by4, kays(A["w_o_2"][0], 4, 4), Freed(o_done, 4))])
        stream.segment(moe2_tiles(main2, "moe2"), GROUPS2)
        stream.segment([fixed("ple", lambda s: by4(s)[:, 0:2, :], kays(A["w_ple_2"][0], 0, 2), Freed(pw_done, 2)),
                        fixed("pg0", by4, kays(A["w_pg_2"][0], 0, 4), Freed(pg_done, 2)),
                        fixed("pg1", by4, kays(A["w_pg_2"][0], 4, 4), Freed(pg_done, 4))])

        restream1 = Stream(rest_landed[0])
        restream1.segment(moe_tiles(rest1, "moe"), EXPERTS * (PASSES - 1))
        restream2 = Stream(rest_landed[1])
        restream2.segment(moe2_tiles(rest2, "moe2"), GROUPS2 * (PASSES - 1))

        block = ctx.enter_context(nc.Block())

        @block.sync
        def _(sp):
            sp.dma_start(x[:], A["x"][0].rearrange("(t p) d -> p t d", p=P)).then_inc(x_landed, 16)

            def load(st, s, tile, i, at):
                for dst, src in tile[2](i, s):
                    sp.dma_start(dst, src).then_inc(st.landed[s], 16)

            def straight(st, k):
                t0, tiles, trips = st.segments[k]
                n = len(tiles)
                if k:
                    _, before, turns = st.segments[k - 1]
                first = tiles if trips == 1 else tiles[:SLOTS]
                for j, tile in enumerate(first):
                    if j >= SLOTS:
                        tiles[j - SLOTS][3].wait(sp)
                    elif k:
                        prev = before[len(before) - SLOTS + j]
                        prev[3].wait(sp, turns - 1 if turns > 1 else None)
                    load(st, (t0 + j) % SLOTS, tile, 0, j)

            def looped(st, k):
                t0, tiles, trips = st.segments[k]
                n = len(tiles)
                with sp.Fori(0, trips - 1) as i:
                    for j in range(SLOTS, n + SLOTS):
                        tiles[j - SLOTS][3].wait(sp, i)
                        load(st, (t0 + j) % SLOTS, tiles[j % n], i if j < n else i + 1, j)
                for j in range(SLOTS, n):
                    tiles[j - SLOTS][3].wait(sp, trips - 1)
                    load(st, (t0 + j) % SLOTS, tiles[j], trips - 1, j)

            def rest(st, passes_of, n_over, main_freed, rest_freed):
                sp.wait_ge(over_ready, n_over)
                more = sp.value_load(over[0:1, n_over - 1:n_over], min_val=0, max_val=1)
                with sp.If(more == 1):
                    main_freed.wait(sp)
                    t0, tiles, trips = st.segments[0]
                    n = len(tiles)
                    for j in range(n):
                        if j >= SLOTS:
                            tiles[j - SLOTS][3].wait(sp, 0)
                        load(st, j % SLOTS, tiles[j], 0, j)
                    for r in range(PASSES - 1):
                        with sp.Fori(0 if r else 1, passes_of) as e:
                            for j in range(n):
                                turn = e + (r * passes_of if j >= SLOTS else r * passes_of - 1)
                                tiles[(j - SLOTS) % n][3].wait(sp, turn)
                                load(st, j % SLOTS, tiles[j], e, j)
                    rest_freed.wait(sp)
                with sp.Else():
                    sp.nop()
                sp.nop()

            for k in (0, 1, 2, 3):
                straight(stream, k)
            looped(stream, 3)
            rest(restream1, EXPERTS, 1, Freed(main1.down_done, EXPERTS * GROUPS),
                 Freed(rest1.down_done, EXPERTS * GROUPS * (PASSES - 1)))
            straight(stream, 4)
            straight(stream, 5)
            looped(stream, 5)
            rest(restream2, GROUPS2, 2, Freed(main2.down_done, 4 * GROUPS2),
                 Freed(rest2.down_done, 4 * GROUPS2 * (PASSES - 1)))
            straight(stream, 6)
            for t in range(TT):
                sp.wait_ge(x_updated, 14 + t + 1)
                sp.dma_start(out[0, t * P:(t + 1) * P, :], x[:, t, :]).then_inc(stored, 16)
            sp.wait_ge(stored, 16 * TT)

        @block.gpsimd
        def _(pool):
            n = [0]

            def link(ins):
                ins.then_inc(consts_step, 1)
                n[0] += 1
                pool.wait_ge(consts_step, n[0])

            def row_gain(k):
                names = [("norm_mix", 0), ("norm_ffn", 0), ("norm_mix", 1), ("norm_ffn", 1), ("norm_final", None),
                         ("attn_norm_g_2", 0), ("ffn_norm_g_2", 0), ("ple_norm_g_2", 0)]
                name, l = names[k]
                g = A[name] if l is None else A[name][l]
                return g.rearrange("(a d) -> a d", a=1).broadcast_to([P, D])

            link(nc.gpsimd.memset(ident[:], 0.0))
            link(nc.gpsimd.affine_select(out=ident[:], in_=ident[:], compare_op=ALU.not_equal, fill=1.0, base=0,
                                         pattern=[[-1, P]], channel_multiplier=1))
            for k in range(2):
                pool.dma_start(gain[:, k, :], row_gain(k)).then_inc(gain_landed[k], 16)
            link(nc.gpsimd.memset(half_c[:], -0.5))
            link(nc.gpsimd.memset(eps_c[:], EPS))
            link(nc.gpsimd.memset(cpad[:], 0.0))
            link(nc.gpsimd.memset(block64[:], 0.0))
            link(nc.gpsimd.memset(block64[0:64, 0:64], 1.0 / 64))
            link(nc.gpsimd.memset(block64[64:128, 64:128], 1.0 / 64))
            pool.wait_ge(sgu_landed, 32)
            for l in range(2):
                w = wk[l][:, 0:512].rearrange("p (h s) -> p h s", h=4)
                nc.gpsimd.affine_select(out=w, in_=w, compare_op=ALU.is_ge, fill=0.0, base=0,
                                        pattern=[[0, 4], [-1, P]], channel_multiplier=1).then_inc(sgu_masked, 1)
            link(nc.gpsimd.memset(ones[:], 1.0))
            link(nc.gpsimd.affine_select(out=upper[:], in_=ones[:], compare_op=ALU.is_ge, fill=0.0, base=0,
                                         pattern=[[1, P]], channel_multiplier=-1))
            link(nc.gpsimd.affine_select(out=above[:], in_=ones[:], compare_op=ALU.is_ge, fill=0.0, base=-1,
                                         pattern=[[1, P]], channel_multiplier=-1))
            link(nc.gpsimd.memset(causal[:], 0.0))
            link(nc.gpsimd.affine_select(out=causal[:, P:], in_=causal[:, P:], compare_op=ALU.is_ge, fill=NEG, base=0,
                                         pattern=[[-1, P]], channel_multiplier=1))
            link(nc.gpsimd.memset(tie[:], 1.0))
            link(nc.gpsimd.affine_select(out=tie[:], in_=tie[:], compare_op=ALU.is_ge, fill=0.0, base=-1,
                                         pattern=[[1, EXPERTS], [-1, EXPERTS]], channel_multiplier=0))
            link(nc.gpsimd.memset(head_row[:], 1.0))
            link(nc.gpsimd.affine_select(out=head_row[:], in_=head_row[:], compare_op=ALU.is_equal, fill=0.0, base=0,
                                         pattern=[[-1, HEADS], [0, P]], channel_multiplier=1))
            link(nc.gpsimd.iota(slot_i[:], pattern=[[1, CAP]], base=0, channel_multiplier=0))
            link(nc.gpsimd.tensor_copy(slot_no[:], slot_i[:]))
            link(nc.gpsimd.memset(negc[:], 0.0))
            link(nc.gpsimd.memset(table[:], 0.0))
            nc.gpsimd.memset(table2[:], 0.0).then_inc(consts_made, 1)
            asks = ["norm", "sgu", "norm", "norm", "sgu", "norm", "norm", "norm", "norm", "norm"]
            norm = 0
            for k, kind in enumerate(asks):
                m = 8 if kind == "sgu" else 2
                pool.wait_ge(ms_ready, k + 1)
                nc.gpsimd.tensor_tensor(rstd[:, 0:m], ms[:, 0:m], half_c[:, 0:m], ALU.pow).then_inc(rstd_ready, 1)
                if kind == "norm":
                    norm += 1
                    if norm + 1 < 8:
                        pool.wait_ge(norm_applied, 2 * norm)
                        b = (norm + 1) % 2
                        pool.dma_start(gain[:, b, :], row_gain(norm + 1)).then_inc(gain_landed[b], 16)

        @block.scalar
        def _(act):
            for l in range(2):
                act.dma_start(wk[l][:, 0:512].rearrange("p (h s) -> p h s", h=4),
                              A["sgu_w"][l].rearrange("h t s -> t h s")).then_inc(sgu_landed, 16)
            r = 0
            for name in ("conv_b", "conv_ng", "conv_nb"):
                act.dma_start(rows[r:r + 8, :], A[name].rearrange("l (c p) -> (l c) p", p=P)).then_inc(rows_landed, 16)
                r += 8
            act.dma_start(rows[r:r + 12, :],
                          A["conv_w_2"][0].rearrange("w (c p) -> (w c) p", p=P)).then_inc(rows_landed, 16)
            r += 12
            for name in ("q_norm_g_2", "k_norm_g_2"):
                for half in range(2):
                    act.dma_start(rows[r:r + 1, 64 * half:64 * half + 64], A[name]).then_inc(rows_landed, 16)
                r += 1
            for l in range(2):
                act.dma_start(rowsw[:, l, :],
                              A["conv_w"][l].rearrange("w a (c p) -> (w a c) p", p=P)).then_inc(rows_landed, 16)
            for l in range(2):
                act.dma_start(sgb[:, l].rearrange("p h t -> p (h t)"),
                              A["sgu_b"][l:l + 1].rearrange("a h t -> a (h t)").broadcast_to([P, 512])
                              ).then_inc(small_landed, 16)
                act.dma_start(sng[:, l, :], A["sgu_ng"][l:l + 1, :].broadcast_to([P, HALF])).then_inc(small_landed, 16)
                act.dma_start(snb[:, l, :], A["sgu_nb"][l:l + 1, :].broadcast_to([P, HALF])).then_inc(small_landed, 16)
            act.dma_start(router1[:], A["moe_router"][0].rearrange("(k p) n -> p k n", p=P)).then_inc(small_landed, 16)
            act.dma_start(router2[:, :, 0:4], A["w_rg_2"][0].rearrange("(k p) n -> p k n", p=P)).then_inc(small_landed, 16)
            act.dma_start(router2[:, :, 4:20], A["w_re_2"][0].rearrange("(k p) n -> p k n", p=P)).then_inc(small_landed, 16)
            act.dma_start(wf[:], cols(w2, 1536, HEADS)).then_inc(small_landed, 16)
            act.dma_start(bias2[:, 0:4], A["b_rg_2"].broadcast_to([P, 4])).then_inc(small_landed, 16)
            act.dma_start(bias2[:, 4:20], A["b_re_2"].broadcast_to([P, 16])).then_inc(small_landed, 16)
            act.dma_start(bf[:], A["b_f_2"].broadcast_to([P, HEADS])).then_inc(small_landed, 16)
            act.dma_start(ptok[:], A["p_2"][0, 0].rearrange("(t p) d -> p t d", p=P)).then_inc(small_landed, 16)

            def norm(n, turn=True):
                if n == 0:
                    act.wait_ge(x_landed, 16)
                else:
                    act.wait_ge(x_updated, 2 * n - 1)
                act.activation(h[:, 0, :], x[:, 0, :], ACT.Square, accum_out=ss[:, 0:1]).then_inc(sumsq_ready, 1)
                if turn:
                    k = n if n < 4 else n - 1
                    for t in range(TT):
                        act.wait_ge(h_turned, 4 * k + 2 * t + 1)
                        act.activation(hT[:, 0:4, t * P:(t + 1) * P],
                                       bank(2 * t).rearrange("p (c s) -> p c s", c=4),
                                       ACT.Copy).then_inc(hT_by_scalar, 1)

            def mixer(l):
                act.wait_ge(proj_done, 4 * l + 1)
                act.activation(wk[0][:], bank(0, 2), ACT.Sigmoid).then_inc(gate_act, 1)
                act.wait_ge(proj_done, 4 * l + 3)
                act.activation(vn[:].rearrange("p t n -> p (t n)"), bank(4, 2), ACT.Gelu).then_inc(v_act, 1)
                act.wait_ge(proj_done, 4 * l + 4)
                act.activation(uT[:].rearrange("p c s -> p (c s)"), bank(6, 2), ACT.Gelu).then_inc(u_act, 1)
                act.wait_ge(v_centred, l + 1)
                act.activation(wk[3][:], vn[:].rearrange("p t n -> p (t n)"), ACT.Square).then_inc(v_squared, 1)
                act.wait_ge(centred, l + 1)
                act.activation(wk[2][:], wk[1][:], ACT.Square).then_inc(squared, 1)
                act.wait_ge(var_done, l + 1)
                act.activation(wk[2][:], bank(2, 2), ACT.Sqrt, bias=eps_c[:, 0:1]).then_inc(std_done, 1)
                act.wait_ge(conv_hat, l + 1)
                act.wait_ge(params_ready, 2)
                for c in range(CH):
                    act.activation(yT[:, c, :], wk[1][:, c * S:(c + 1) * S], ACT.Silu,
                                   bias=pcol[:, 16 + 4 * l + c:17 + 4 * l + c],
                                   scale=pcol[:, 8 + 4 * l + c:9 + 4 * l + c]).then_inc(conv_act, 1)

            def experts(s, i):
                act.wait_ge(s.gathered, 2 * i + 1)
                act.activation(xg[:, 0:4, :], bank(6)[:, 0:4 * CAP].rearrange("p (c s) -> p c s", c=4), ACT.Copy)
                act.activation(spread[0:CAP, 0:P], PS[0:CAP, 6, 4 * CAP:512], ACT.Copy).then_inc(s.xg_by_scalar, 1)
                for j in range(GROUPS):
                    m = CAP * ffn_chunks(j)
                    act.wait_ge(s.gu_ready, i * GROUPS + (j + 1))
                    if j >= 2:
                        act.wait_ge(s.hid_ready, i * GROUPS + (j - 1))
                    act.activation(wk[j % 2][:, 0:m], bank(j % 2)[:, 0:m], ACT.Silu).then_inc(s.silu_ready, 1)
                act.wait_ge(s.down_done, i * GROUPS + GROUPS)
                act.activation(wk[4][0:CAP, HALF:D], PS[0:CAP, 5, :], ACT.Copy).then_inc(s.y_by_scalar, 1)

            def experts2(s, i):
                act.wait_ge(s.gathered, 2 * i + 1)
                act.activation(xg[:, 0:4, :], bank(6)[:, 0:4 * CAP].rearrange("p (c s) -> p c s", c=4), ACT.Copy)
                act.activation(spread[0:CAP, 0:P], PS[0:CAP, 6, 4 * CAP:512], ACT.Copy).then_inc(s.xg_by_scalar, 1)
                for q in range(4):
                    act.wait_ge(s.gu_ready, i * 4 + (q + 1))
                    if q >= 2:
                        act.wait_ge(s.hid_ready, i * 4 + (q - 1))
                    act.activation(wk[q % 2][:, 0:2 * CAP], bank(q % 2)[:, 0:2 * CAP], ACT.Silu).then_inc(s.silu_ready, 1)

            def route_exps(k, n):
                act.wait_ge(exps_wanted, k)
                act.activation(ex[:, :, 0:n], shifted[:, :, 0:n], ACT.Exp).then_inc(exps_ready, 1)

            act.wait_ge(params_turned, 1)
            act.activation(pcol[:], bank(0)[:, 0:NROW], ACT.Copy)
            act.activation(wcol[:].rearrange("p l w -> p (l w)"), bank(0)[:, NROW:NROW + 2 * CH * TAPS],
                           ACT.Copy).then_inc(params_ready, 1)
            act.wait_ge(params_turned, 2)
            act.activation(wsT[:].rearrange("p l h t -> p (l h t)"), bank(2, 2), ACT.Copy).then_inc(params_ready, 1)
            act.wait_ge(params_turned, 3)
            act.activation(pT[:].rearrange("p k s -> p (k s)"), bank(4), ACT.Copy).then_inc(params_ready, 1)
            norm(0)
            mixer(0)
            norm(1)
            for j in range(11):
                act.wait_ge(gu_ready, j + 1)
                if j >= 2:
                    act.wait_ge(hid_ready, j - 1)
                act.activation(wk[j % 2][:, 0:512], bank(j % 2), ACT.Silu).then_inc(silu_ready, 1)
            norm(2)
            mixer(1)
            norm(3)
            route_exps(1, EXPERTS)
            with act.Fori(0, EXPERTS) as i:
                experts(main1, i)
            act.wait_ge(over_ready, 1)
            more = act.value_load(over[0:1, 0:1], min_val=0, max_val=1)
            with act.If(more == 1):
                with act.Fori(0, EXPERTS * (PASSES - 1)) as i:
                    experts(rest1, i)
            with act.Else():
                act.nop()
            act.nop()
            norm(4, turn=False)
            norm(5)

            act.wait_ge(log_step, ABS_Z)
            act.activation(hs[:, 2:4, :], hs[:, 0:2, :], ACT.Exp, scale=-1.0).then_inc(log_step, 1)
            act.wait_ge(log_step, EXP_Z)
            act.activation(hs[:, 4:6, :], hs[:, 2:4, :], ACT.Ln, bias=ones[:, 0:1]).then_inc(log_step, 1)
            for k in range(2):
                act.wait_ge(proj2, k + 1)
                act.activation(wk[k][:], bank(2 * k, 2), ACT.Square).then_inc(qk_sq, 1)
            act.wait_ge(proj2, 3)
            act.activation(vn[:].rearrange("p t n -> p (t n)"), bank(4, 2), ACT.Copy).then_inc(v2_copied, 1)
            for k in range(2):
                act.wait_ge(qk_ms, k + 1)
                act.activation(wk[2 + k][:], bank(6, 2), ACT.Sqrt, bias=eps_c[:, 0:1]).then_inc(qk_std, 1)
            act.wait_ge(qk_hat, 2)
            act.wait_ge(proj2, 4)
            act.activation(wk[0][:], bank(0, 2), ACT.Copy).then_inc(cbu_copied, 1)
            act.wait_ge(proj2, 6)
            act.activation(wk[1][:], bank(4, 2), ACT.Copy).then_inc(cbu_copied, 1)
            for k, (dst, b) in enumerate(((sgu[:, 0], 0), (sgu[:, 1], 6), (sgu[:, 2], 4), (sgu[:, 3], 0))):
                act.wait_ge(proj2, 7 + k)
                act.activation(dst, bank(b, 2), ACT.Sigmoid).then_inc(gates_act, 1)
            for t in range(TT):
                L = L1 if t else L0
                act.wait_ge(att_max, t + 1)
                for hd in range(HEADS):
                    act.activation(L[:, hd, :], L[:, hd, :], ACT.Exp, bias=negmax[:, t, hd:hd + 1], scale=0.125,
                                   accum_out=rowsum[:, t, hd:hd + 1]).then_inc(att_exp, 1)
                for b in range(0, 2 * (t + 1), 2):
                    act.wait_ge(att_turned, 2 * t + b + 1)
                    act.activation(PT[:, 4 * b:4 * b + 4, :], bank(2 + 2 * t + b).rearrange("p (c s) -> p c s", c=4),
                                   ACT.Copy).then_inc(att_pT_s, 1)
                act.wait_ge(att_yturned, t + 1)
                act.activation(yT[:, 0:4, t * P:(t + 1) * P], bank(1).rearrange("p (c s) -> p c s", c=4),
                               ACT.Copy).then_inc(att_yT, 1)
            norm(6)
            route_exps(2, 20)
            with act.Fori(0, GROUPS2) as i:
                experts2(main2, i)
            act.wait_ge(over_ready, 2)
            more = act.value_load(over[0:1, 1:2], min_val=0, max_val=1)
            with act.If(more == 1):
                with act.Fori(0, GROUPS2 * (PASSES - 1)) as i:
                    experts2(rest2, i)
            with act.Else():
                act.nop()
            act.nop()
            norm(7)
            for t in range(TT):
                act.wait_ge(pg_done, 3 + t)
                act.activation(wk[t], bank(2 * t, 2), ACT.Sigmoid).then_inc(pg_act, 1)

        @block.tensor
        def _(pe):
            mm = nc.tensor.matmul

            def turn(n):
                for t in range(TT):
                    pe.wait_ge(norm_applied, 2 * n + t + 1)
                    for b in range(2):
                        for c in range(4):
                            last = nc.tensor.transpose(PS[:, 2 * t + b, c * P:(c + 1) * P],
                                                       h[:, t, (4 * b + c) * P:(4 * b + c + 1) * P], ident[:])
                        last.then_inc(h_turned, 1)

            def have_hT(n):
                k = n if n < 4 else n - 1
                pe.wait_ge(hT_by_scalar, 2 * k + 2)
                pe.wait_ge(hT_by_vector, 2 * k + 2)

            def project_T(s, b):
                for c in range(4):
                    for k in range(KC):
                        last = mm(chunks(b)[:, c, :], by8(s)[:, k, c * P:(c + 1) * P], hT[:, k, :],
                                  start=(k == 0), stop=(k == KC - 1))
                return last

            def project(s, b):
                for t in range(TT):
                    for k in range(KC):
                        last = mm(bank(b + t), hT[:, k, t * P:(t + 1) * P], by8(s)[:, k, :],
                                  start=(k == 0), stop=(k == KC - 1))
                return last

            def rows_of_model(s, lhs, b, first, last_one, signal, n=4):
                for t in range(TT):
                    for hf in range(2):
                        for k in range(n):
                            last = mm(bank(b + 2 * t + hf), lhs(k)[:, t * P:(t + 1) * P],
                                      by4(s)[:, k, hf * HALF:(hf + 1) * HALF],
                                      start=(first and k == 0), stop=(last_one and k == n - 1))
                    last.then_inc(signal, 1)

            def mixer(l):
                have_hT(2 * l)
                project_T(stream.arrived(pe, (l, "gate")), 0).then_inc(proj_done, 1)
                project_T(stream.arrived(pe, (l, "a")), 2).then_inc(proj_done, 1)
                project(stream.arrived(pe, (l, "v")), 4).then_inc(proj_done, 1)
                project_T(stream.arrived(pe, (l, "u")), 6).then_inc(proj_done, 1)
                pe.wait_ge(conv_done, l + 1)
                for b in range(2):
                    last = mm(bank(b), block64[:], wk[1][:, b * HALF:(b + 1) * HALF], start=True, stop=True)
                last.then_inc(mean_done, 1)
                pe.wait_ge(v_ready, l + 1)
                for hd in range(4):
                    for n in range(TT):
                        last = mm(chunks(4)[:, hd, n * P:(n + 1) * P], vn[:, n, hd * P:(hd + 1) * P], wsT[:, l, hd, :],
                                  start=True, stop=True)
                last.then_inc(mixed, 1)
                pe.wait_ge(squared, l + 1)
                for b in range(2):
                    last = mm(bank(2 + b), block64[:], wk[2][:, b * HALF:(b + 1) * HALF], start=True, stop=True)
                last.then_inc(var_done, 1)
                pe.wait_ge(sgu_out, l + 1)
                rows_of_model(stream.arrived(pe, (l, "out_sgu")), lambda k: yT[:, 4 + k, :], 4, True, False, out_done)
                pe.wait_ge(conv_act, 4 * (l + 1))
                rows_of_model(stream.arrived(pe, (l, "out_conv")), lambda k: yT[:, k, :], 4, False, True, out_done)

            def dense():
                have_hT(1)

                def gate_up(j):
                    if j >= 2:
                        pe.wait_ge(hid_ready, j - 1)
                    for b, kind in ((j % 2, "g"), (2 + j % 2, "u")):
                        s = stream.arrived(pe, ("ffn", kind, j // 2))
                        for c in range(2):
                            f = (2 * (j % 2) + c) * P
                            for k in range(KC):
                                last = mm(chunks(b, 1)[:, c, :], by8(s)[:, k, f:f + P], hT[:, k, :],
                                          start=(k == 0), stop=(k == KC - 1))
                    last.then_inc(gu_ready, 1)

                def down(j):
                    pe.wait_ge(hid_ready, j + 1)
                    s = stream.arrived(pe, ("ffn", "d", j // 2))
                    for t in range(TT):
                        for hf in range(2):
                            for c in range(2):
                                last = mm(bank(4 + 2 * t + hf), wk[2 + j % 2][:, c * S + t * P:c * S + (t + 1) * P],
                                          by4(s)[:, 2 * (j % 2) + c, hf * HALF:(hf + 1) * HALF],
                                          start=(j == 0 and c == 0), stop=(j == 10 and c == 1))
                    last.then_inc(down_done, 1)

                gate_up(0)
                for j in range(1, 11):
                    gate_up(j)
                    down(j - 1)
                down(10)

            def route(n, weights, ne, groups, k):
                have_hT(n)
                if k == 1:
                    pe.wait_ge(small_landed, 16 * 14)
                for t in range(TT):
                    for c in range(KC):
                        last = mm(PS[:, 0, t * ne:(t + 1) * ne], hT[:, c, t * P:(t + 1) * P], weights[:, c, :],
                                  start=(c == 0), stop=(c == KC - 1))
                last.then_inc(logits_ready, 1)
                pe.wait_ge(mask_ready, k)
                m = [mk[:, t, 0:groups] for t in range(TT)]
                mm(PS[:, 1, 0:groups], above[:], m[0], start=True, stop=True)
                mm(PS[:, 1, groups:2 * groups], ones[:], m[0], start=True, stop=False)
                mm(PS[:, 1, groups:2 * groups], above[:], m[1], start=False, stop=True)
                mm(PS[:, 1, 2 * groups:3 * groups], ones[:], m[0], start=True, stop=False)
                mm(PS[:, 1, 2 * groups:3 * groups], ones[:], m[1], start=False, stop=True).then_inc(rank_ready, 1)

            def gather(s, i, turned, extra=None):
                pe.wait_ge(s.picked, i + 1)
                pe.wait_ge(s.added, i * 4 + 1)
                for b in range(2):
                    for c in range(4):
                        for t in range(TT):
                            mm(PS[:, 6 + b, c * CAP:(c + 1) * CAP], h[:, t, (4 * b + c) * P:(4 * b + c + 1) * P],
                               pick[:, t, :], start=(t == 0), stop=(t == TT - 1))
                    last = nc.tensor.transpose(PS[0:CAP, 6 + b, 4 * CAP:512], turned[:, b, :], ident[:])
                    if b and extra:
                        last = extra()
                    last.then_inc(s.gathered, 1)
                pe.wait_ge(s.xg_by_scalar, i + 1)
                pe.wait_ge(s.xg_by_vector, i + 1)

            def scatter(s, i):
                for t in range(TT):
                    for hf in range(2):
                        if t:
                            pe.wait_ge(s.added, i * 4 + (hf + 2))
                        mm(bank(6 + hf), spread[0:CAP, t * P:(t + 1) * P], wk[4][0:CAP, hf * HALF:(hf + 1) * HALF],
                           start=True, stop=True).then_inc(s.scattered, 1)

            def experts(st, s, i):
                gather(s, i, pickg)

                def gate_up(j):
                    if j >= 2:
                        pe.wait_ge(s.hid_ready, i * GROUPS + (j - 1))
                    for b, kind in ((j % 2, "g"), (2 + j % 2, "u")):
                        w = st.arrived(pe, ("moe", kind, j), i)
                        for c in range(ffn_chunks(j)):
                            for k in range(KC):
                                last = mm(PS[:, b, c * CAP:(c + 1) * CAP], by8(w)[:, k, c * P:(c + 1) * P],
                                          xg[:, k, :], start=(k == 0), stop=(k == KC - 1))
                    last.then_inc(s.gu_ready, 1)

                def down(j):
                    pe.wait_ge(s.hid_ready, i * GROUPS + (j + 1))
                    w = st.arrived(pe, ("moe", "d", j), i)
                    n = ffn_chunks(j)
                    for hf in range(2):
                        for c in range(n):
                            last = mm(PS[0:CAP, 4 + hf, :], wk[2 + j % 2][:, c * CAP:(c + 1) * CAP],
                                      by4(w)[:, c, hf * HALF:(hf + 1) * HALF],
                                      start=(j == 0 and c == 0), stop=(j == GROUPS - 1 and c == n - 1))
                    last.then_inc(s.down_done, 1)

                gate_up(0)
                for j in range(1, GROUPS):
                    gate_up(j)
                    down(j - 1)
                down(GROUPS - 1)
                pe.wait_ge(s.y_by_scalar, i + 1)
                pe.wait_ge(s.y_by_vector, i + 1)
                scatter(s, i)

            def experts2(st, s, i):
                def gates():
                    for t in range(TT):
                        last = mm(PS[0:CAP, 0, 4 * CAP:4 * CAP + 4], pick[:, t, :], now2[:, 2:6, t],
                                  start=(t == 0), stop=(t == TT - 1))
                    return last

                gather(s, i, pick, gates)

                def gate_up(q):
                    if q >= 2:
                        pe.wait_ge(s.hid_ready, i * 4 + (q - 1))
                    w = st.arrived(pe, ("moe2", "gu", q), i)
                    tile = slot(w).rearrange("p (w k n) -> p w k n", w=2, k=KC)
                    for m in range(2):
                        for c in range(2):
                            for k in range(KC):
                                last = mm(PS[:, q % 2, (2 * m + c) * CAP:(2 * m + c + 1) * CAP],
                                          tile[:, m, k, c * P:(c + 1) * P], xg[:, k, :],
                                          start=(k == 0), stop=(k == KC - 1))
                    last.then_inc(s.gu_ready, 1)

                def down(q):
                    pe.wait_ge(s.hid_ready, i * 4 + (q + 1))
                    if q >= 2:
                        pe.wait_ge(s.y_by_vector, i * 4 + (q - 1))
                    w = st.arrived(pe, ("moe2", "d", q - q % 2), i)
                    tile = slot(w).rearrange("p (e k n) -> p e k n", e=2, k=2)
                    for hf in range(2):
                        for c in range(2):
                            last = mm(PS[0:CAP, 2 + 2 * (q % 2) + hf, :], wk[2 + q % 2][:, c * CAP:(c + 1) * CAP],
                                      tile[:, q % 2, c, hf * HALF:(hf + 1) * HALF], start=(c == 0), stop=(c == 1))
                    last.then_inc(s.down_done, 1)

                gate_up(0)
                for q in range(1, 4):
                    gate_up(q)
                    down(q - 1)
                down(3)
                pe.wait_ge(s.y_by_vector, i * 4 + 4)
                scatter(s, i)

            def sweeps(body, main, rest_s, st_rest, n, k):
                with pe.Fori(0, n) as i:
                    body(stream, main, i)
                pe.wait_ge(over_ready, k)
                more = pe.value_load(over[0:1, k - 1:k], min_val=0, max_val=1)
                with pe.If(more == 1):
                    with pe.Fori(0, n * (PASSES - 1)) as i:
                        body(st_rest, rest_s, i)
                with pe.Else():
                    pe.nop()
                pe.nop()

            pe.wait_ge(consts_made, 1)
            pe.wait_ge(rows_landed, 16 * 10)
            nc.tensor.transpose(PS[:, 0, 0:NROW], rows, ident[0:NROW, 0:NROW])
            for l in range(2):
                w = CH * TAPS
                last = nc.tensor.transpose(PS[:, 0, NROW + l * w:NROW + (l + 1) * w], rowsw[:, l, :], ident[0:w, 0:w])
            last.then_inc(params_turned, 1)
            pe.wait_ge(sgu_masked, 2)
            for l in range(2):
                for hd in range(4):
                    last = nc.tensor.transpose(PS[:, 2 + l, hd * P:(hd + 1) * P], wk[l][:, hd * P:(hd + 1) * P], ident[:])
            last.then_inc(params_turned, 1)
            pe.wait_ge(small_landed, 16 * 14)
            for k in range(2):
                for t in range(TT):
                    last = nc.tensor.transpose(PS[:, 4, k * S + t * P:k * S + (t + 1) * P],
                                               ptok[:, t, k * P:(k + 1) * P], ident[:])
            last.then_inc(params_turned, 1)
            pe.wait_ge(params_ready, 3)
            turn(0)
            mixer(0)
            turn(1)
            dense()
            turn(2)
            mixer(1)
            turn(3)
            route(3, router1, EXPERTS, EXPERTS, 1)
            sweeps(experts, main1, rest1, restream1, EXPERTS, 1)
            turn(5)
            have_hT(5)

            for t in range(TT):
                for c in range(KC):
                    last = mm(PS[:, 6, t * HEADS:(t + 1) * HEADS], hT[:, c, t * P:(t + 1) * P], wf[:, c, :],
                              start=(c == 0), stop=(c == KC - 1))
            last.then_inc(f_ready, 1)
            project_T(stream.arrived(pe, "q"), 0).then_inc(proj2, 1)
            project_T(stream.arrived(pe, "k"), 2).then_inc(proj2, 1)
            project(stream.arrived(pe, "v"), 4).then_inc(proj2, 1)
            pe.wait_ge(log_step, LOG_F)
            mm(PS[:, 7, 0:8], upper[:], lf[:, 0, :], start=True, stop=True)
            mm(PS[:, 7, 8:16], ones[:], lf[:, 0, :], start=True, stop=False)
            mm(PS[:, 7, 8:16], upper[:], lf[:, 1, :], start=False, stop=True)
            mm(PS[0:HEADS, 7, 128:256], lf[:, 0, :], upper[:], start=True, stop=True)
            mm(PS[0:HEADS, 7, 256:384], lf[:, 0, :], ones[:], start=True, stop=False)
            mm(PS[0:HEADS, 7, 256:384], lf[:, 1, :], upper[:], start=False, stop=True).then_inc(cum_ready, 1)
            pe.wait_ge(cum_copied, 1)
            for w in range(2):
                pe.wait_ge(qk_sq, w + 1)
                if w:
                    pe.wait_ge(qk_std, 1)
                for b in range(2):
                    last = mm(bank(6 + b), block64[:], wk[w][:, b * HALF:(b + 1) * HALF], start=True, stop=True)
                last.then_inc(qk_ms, 1)
            for name, b, freed, value in (("cb", 0, qk_hat, 1), ("cc", 2, qk_hat, 2), ("cu", 4, v2_copied, 1),
                                          ("ga0", 0, cbu_copied, 1), ("ga1", 6, qk_std, 2), ("gb0", 4, cbu_copied, 2),
                                          ("gb1", 0, gates_act, 1)):
                pe.wait_ge(freed, value)
                project_T(stream.arrived(pe, name), b).then_inc(proj2, 1)
            pe.wait_ge(cc_used, 1)
            pe.wait_ge(gates_act, 4)
            for t in range(TT):
                n, each = P * (t + 1), 4 // (t + 1)
                for hd in range(HEADS):
                    o = PS[:, 2 + 2 * t + hd // each, (hd % each) * n:(hd % each + 1) * n]
                    mm(o, qz[:, hd, t * P:(t + 1) * P], uT[:, hd // 2, 0:n], start=True, stop=False)
                    last = mm(o, head_row[:, hd, :], negc[:, 0:n], start=False, stop=True)
                last.then_inc(att_logits, 1)
            for t in range(TT):
                L, nk = (L1 if t else L0), t + 1
                pe.wait_ge(att_exp, HEADS * (t + 1))
                for b in range(2 * nk):
                    for c in range(4):
                        hd, kt = (4 * b + c) // nk, (4 * b + c) % nk
                        last = nc.tensor.transpose(PS[:, 2 + 2 * t + b, c * P:(c + 1) * P],
                                                   L[:, hd, kt * P:(kt + 1) * P], ident[:])
                    last.then_inc(att_turned, 1)
                pe.wait_ge(att_pT_s, (1, 3)[t])
                pe.wait_ge(att_pT_v, (1, 3)[t])
                for hd in range(HEADS):
                    for kt in range(nk):
                        last = mm(PS[:, 0, hd * 64:(hd + 1) * 64], PT[:, hd * nk + kt, :], vn[:, kt, hd * 64:(hd + 1) * 64],
                                  start=(kt == 0), stop=(kt == nk - 1))
                last.then_inc(att_out, 1)
                pe.wait_ge(att_y, t + 1)
                if t:
                    pe.wait_ge(att_yT, t)
                for c in range(4):
                    last = nc.tensor.transpose(PS[:, 1, c * P:(c + 1) * P], wk[2 + t][:, c * P:(c + 1) * P], ident[:])
                last.then_inc(att_yturned, 1)
            for k, (name, b, half) in enumerate((("out_att", 0, 0), ("out_conv2", 4, 4))):
                if k == 0:
                    pe.wait_ge(att_yT, 2)
                else:
                    pe.wait_ge(yconv, 1)
                s = stream.arrived(pe, name)
                for c in range(KC):
                    for kk in range(4):
                        last = mm(chunks(b, 4)[:, c, :], by4(s)[:, kk, c * P:(c + 1) * P], yT[:, half + kk, :],
                                  start=(kk == 0), stop=(kk == 3))
                    if c % 4 == 3:
                        last.then_inc(merge_mm, 1)
            mT = sgu[:, 0:2, :].rearrange("p a (c s) -> p (a c) s", s=S)
            pe.wait_ge(merged, 2)
            rows_of_model(stream.arrived(pe, "o0"), lambda k: mT[:, k, :], 0, True, False, o_done)
            rows_of_model(stream.arrived(pe, "o1"), lambda k: mT[:, 4 + k, :], 0, False, True, o_done)
            turn(6)
            route(6, router2, 20, GROUPS2, 2)
            sweeps(experts2, main2, rest2, restream2, GROUPS2, 2)
            pe.wait_ge(x_updated, 14)
            rows_of_model(stream.arrived(pe, "ple"), lambda k: pT[:, k, :], 4, True, True, pw_done, 2)
            turn(7)
            have_hT(7)
            rows_of_model(stream.arrived(pe, "pg0"), lambda k: hT[:, k, :], 0, True, False, pg_done)
            rows_of_model(stream.arrived(pe, "pg1"), lambda k: hT[:, 4 + k, :], 0, False, True, pg_done)

        @block.vector
        def _(v):
            own = Own(v, vstep)
            tt, ts, stt = nc.vector.tensor_tensor, nc.vector.tensor_scalar, nc.vector.scalar_tensor_tensor
            copy = nc.vector.tensor_copy
            asked = [0]

            def rsqrt(n):
                asked[0] += 1
                v.wait_ge(rstd_ready, asked[0])

            def updated():
                for t in range(TT):
                    nc.vector.memset(tick[:, t:t + 1], 0.0).then_inc(x_updated, 1)

            def norm(n, turned=True):
                if n == 0:
                    v.wait_ge(x_landed, 16)
                else:
                    v.wait_ge(x_updated, 2 * n)
                own.link(nc.vector.tensor_tensor_reduce(h[:, 1, :], x[:, 1, :], x[:, 1, :], 1.0, 0.0, ALU.mult,
                                                        ALU.add, ss[:, 1:2]))
                v.wait_ge(sumsq_ready, n + 1)
                ts(ms[:, 0:2], ss[:], 1.0 / D, EPS, ALU.mult, ALU.add).then_inc(ms_ready, 1)
                rsqrt(2)
                v.wait_ge(gain_landed[n % 2], 16 * (n // 2 + 1))
                dst = h if turned else x
                for t in range(TT):
                    stt(out=dst[:, t, :], in0=x[:, t, :], scalar=rstd[:, t:t + 1], in1=gain[:, n % 2, :],
                        op0=ALU.mult, op1=ALU.mult).then_inc(norm_applied, 1)
                if turned:
                    k = n if n < 4 else n - 1
                    for t in range(TT):
                        v.wait_ge(h_turned, 4 * k + 2 * t + 2)
                        copy(hT[:, 4:8, t * P:(t + 1) * P],
                             bank(2 * t + 1).rearrange("p (c s) -> p c s", c=4)).then_inc(hT_by_vector, 1)

            def add_rows(b, signal, base):
                for t in range(TT):
                    v.wait_ge(signal, base + t)
                    tt(x[:, t, :], x[:, t, :], bank(b + 2 * t, 2), ALU.add).then_inc(x_updated, 1)

            def mixer(l):
                flat_v = vn[:].rearrange("p t n -> p (t n)")
                by_head = flat_v.rearrange("p (a n) -> p a n", n=P)
                acc = wk[1].rearrange("p (c s) -> p c s", c=CH)
                v.wait_ge(proj_done, 4 * l + 2)
                v.wait_ge(gate_act, l + 1)
                own.link(tt(cpad[:, :, PAD:], chunks(2), wk[0].rearrange("p (c s) -> p c s", c=CH), ALU.mult))
                v.wait_ge(params_ready, 3)
                for k in range(TAPS):
                    for c in range(CH):
                        w = wcol[:, l, 4 * k + c:4 * k + c + 1]
                        if k == 0:
                            ins = ts(acc[:, c, :], cpad[:, c, 0:S], w, pcol[:, 4 * l + c:4 * l + c + 1],
                                     ALU.mult, ALU.add)
                        else:
                            own.settle(behind=CH - 1)
                            ins = stt(out=acc[:, c, :], in0=cpad[:, c, k:k + S], scalar=w, in1=acc[:, c, :],
                                      op0=ALU.mult, op1=ALU.add)
                        if k == TAPS - 1 and c == CH - 1:
                            ins.then_inc(conv_done, 1)
                        else:
                            own.mark(ins)
                v.wait_ge(conv_done, l + 1)
                v.wait_ge(v_act, l + 1)
                v.wait_ge(small_landed, 16 * 14)
                own.link(nc.vector.tensor_reduce(s8[:], by_head, AX_X, ALU.add))
                own.link(ts(s8[:], s8[:], 1.0 / P, None, ALU.mult))
                tt(by_head, by_head, s8[:].unsqueeze(2).to_broadcast([P, 8, P]), ALU.subtract).then_inc(v_centred, 1)
                v.wait_ge(mean_done, l + 1)
                tt(wk[1], wk[1], bank(0, 2), ALU.subtract).then_inc(centred, 1)
                v.wait_ge(v_squared, l + 1)
                own.link(nc.vector.tensor_reduce(s8[:], wk[3].rearrange("p (a n) -> p a n", n=P), AX_X, ALU.add))
                ts(ms[:], s8[:], 1.0 / P, EPS, ALU.mult, ALU.add).then_inc(ms_ready, 1)
                rsqrt(8)
                own.link(tt(by_head, by_head, rstd[:].unsqueeze(2).to_broadcast([P, 8, P]), ALU.mult))
                own.link(tt(vn[:], vn[:], sng[:, l, :].unsqueeze(1).to_broadcast([P, TT, HALF]), ALU.mult))
                tt(vn[:], vn[:], snb[:, l, :].unsqueeze(1).to_broadcast([P, TT, HALF]), ALU.add).then_inc(v_ready, 1)
                v.wait_ge(std_done, l + 1)
                own.link(nc.vector.reciprocal(wk[2], wk[2]))
                tt(wk[1], wk[1], wk[2], ALU.mult).then_inc(conv_hat, 1)
                v.wait_ge(mixed, l + 1)
                v.wait_ge(u_act, l + 1)
                m4 = PS[:, 4:6, :].rearrange("p b (h n t) -> p (b h) n t", n=TT, t=P)
                w4 = wk[0].rearrange("p (h n t) -> p h n t", h=4, n=TT)
                for n in range(TT):
                    own.link(tt(w4[:, :, n, :], m4[:, :, n, :], sgb[:, l], ALU.add))
                tt(yT[:, 4:8, :], uT[:], wk[0].rearrange("p (c s) -> p c s", c=CH), ALU.mult).then_inc(sgu_out, 1)
                add_rows(4, out_done, 4 * l + 3)

            def dense():
                for j in range(11):
                    v.wait_ge(silu_ready, j + 1)
                    if j >= 2:
                        v.wait_ge(down_done, j - 1)
                    tt(wk[2 + j % 2][:, 0:512], wk[j % 2][:, 0:512], bank(2 + j % 2), ALU.mult).then_inc(hid_ready, 1)
                v.wait_ge(down_done, 11)
                for t in range(TT):
                    tt(x[:, t, :], x[:, t, :], bank(4 + 2 * t, 2), ALU.add).then_inc(x_updated, 1)

            def places(values, rows_, n, dst):
                shape = [P, rows_, n, n]
                gt = pair_gt[:, 0:rows_ * n * n].rearrange("p (r i j) -> p r i j", i=n, j=n)
                eq = pair_eq[:, 0:rows_ * n * n].rearrange("p (r i j) -> p r i j", i=n, j=n)
                other, self_ = values.unsqueeze(2).to_broadcast(shape), values.unsqueeze(3).to_broadcast(shape)
                own.mark(tt(gt, other, self_, ALU.is_gt))
                own.link(tt(eq, other, self_, ALU.is_equal))
                own.link(tt(eq, eq, tie[:, 0:n, 0:n].unsqueeze(1).to_broadcast(shape), ALU.mult))
                own.link(tt(gt, gt, eq, ALU.add))
                own.link(nc.vector.tensor_reduce(dst, gt, AX_X, ALU.add))

            def over_flag(k, groups):
                own.link(nc.vector.tensor_reduce(over_f[:, 0:1], PS[:, 1, 2 * groups:3 * groups], AX_X, ALU.max))
                own.link(ts(over_f[:, 1:2], over_f[:, 0:1], float(CAP), None, ALU.is_gt))
                copy(over[0:1, k - 1:k], over_f[0:1, 1:2]).then_inc(over_ready, 1)

            def route():
                v.wait_ge(logits_ready, 1)
                l8, m8 = lg[:, :, 0:EXPERTS], mk[:, :, 0:EXPERTS]
                own.link(copy(l8, PS[:, 0, 0:TT * EXPERTS].rearrange("p (t e) -> p t e", t=TT)))
                own.link(nc.vector.tensor_reduce(mx[:, 0:TT], l8, AX_X, ALU.max))
                tt(shifted[:, :, 0:EXPERTS], l8, mx[:, 0:TT].unsqueeze(2).to_broadcast([P, TT, EXPERTS]),
                   ALU.subtract).then_inc(exps_wanted, 1)
                places(l8, TT, EXPERTS, cnt[:, :, 0:EXPERTS])
                ts(m8, cnt[:, :, 0:EXPERTS], 1.5, None, ALU.is_lt).then_inc(mask_ready, 1)
                v.wait_ge(mask_ready, 1)
                v.wait_ge(exps_ready, 1)
                e8 = ex[:, :, 0:EXPERTS]
                own.link(tt(e8, e8, m8, ALU.mult))
                own.link(nc.vector.tensor_reduce(den[:, 0:TT], e8, AX_X, ALU.add))
                own.link(nc.vector.reciprocal(den[:, 0:TT], den[:, 0:TT]))
                own.link(tt(e8, e8, den[:, 0:TT].unsqueeze(2).to_broadcast([P, TT, EXPERTS]), ALU.mult))
                v.wait_ge(rank_ready, 1)
                rank = PS[:, 1, 0:TT * EXPERTS].rearrange("p (t e) -> p e t", t=TT)
                for p in range(PASSES):
                    c = slice(p * EXPERTS, (p + 1) * EXPERTS)
                    own.mark(ts(table[:, c, 0, :], rank, float(-p * CAP), None, ALU.add))
                    own.mark(copy(table[:, c, 1, :], m8.rearrange("p t e -> p e t")))
                    own.mark(copy(table[:, c, 2, :], e8.rearrange("p t e -> p e t")))
                over_flag(1, EXPERTS)

            def route2():
                v.wait_ge(logits_ready, 2)
                own.link(tt(lg[:], PS[:, 0, 0:TT * 20].rearrange("p (t e) -> p t e", t=TT),
                            bias2[:].unsqueeze(1).to_broadcast([P, TT, 20]), ALU.add))
                four = lambda a: a.rearrange("p t (g e) -> p t g e", e=4)
                own.link(nc.vector.tensor_reduce(den[:], four(lg[:]), AX_X, ALU.max))
                tt(four(shifted[:]), four(lg[:]),
                   den[:].rearrange("p (t g) -> p t g", t=TT).unsqueeze(3).to_broadcast([P, TT, 5, 4]),
                   ALU.subtract).then_inc(exps_wanted, 1)
                for g in range(5):
                    places(lg[:, :, 4 * g:4 * g + 4], TT, 4, cnt[:, :, 4 * g:4 * g + 4])
                own.link(ts(mk[:, :, 4:20], cnt[:, :, 4:20], 1.5, None, ALU.is_lt))
                ts(mk[:, :, 0:4], cnt[:, :, 0:4], 0.5, None, ALU.is_lt).then_inc(mask_ready, 1)
                v.wait_ge(mask_ready, 2)
                v.wait_ge(exps_ready, 2)
                own.link(tt(ex[:, :, 4:20], ex[:, :, 4:20], mk[:, :, 4:20], ALU.mult))
                own.link(nc.vector.tensor_reduce(den[:], four(ex[:]), AX_X, ALU.add))
                own.link(nc.vector.reciprocal(den[:], den[:]))
                d5 = den[:].rearrange("p (t g) -> p t g", t=TT)
                own.link(tt(four(ex[:]), four(ex[:]), d5.unsqueeze(3).to_broadcast([P, TT, 5, 4]), ALU.mult))
                for t in range(TT):
                    own.link(ts(ex[:, t, 4:20], ex[:, t, 4:20], d5[:, t, 0:1], None, ALU.mult))
                v.wait_ge(rank_ready, 2)
                rank = PS[:, 1, 0:TT * GROUPS2].rearrange("p (t e) -> p e t", t=TT)
                for p in range(PASSES):
                    c = slice(p * GROUPS2, (p + 1) * GROUPS2)
                    own.mark(ts(table2[:, c, 0, :], rank, float(-p * CAP), None, ALU.add))
                    own.mark(copy(table2[:, c, 1, :], mk[:, :, 0:4].rearrange("p t e -> p e t")))
                    for t in range(TT):
                        own.mark(copy(table2[:, c, 2:6, t], ex[:, t, 4:20].rearrange("p (g e) -> p g e", e=4)))
                over_flag(2, GROUPS2)

            def choose(s, mine, fields, src, weighted):
                mine.link(copy(fields[:], src))
                for t in range(TT):
                    last = ts(pick[:, t, :], slot_no[:], fields[:, 0, t:t + 1], fields[:, 1, t:t + 1],
                              ALU.is_equal, ALU.mult)
                    if weighted:
                        last = ts(pickg[:, t, :], slot_no[:], fields[:, 0, t:t + 1], fields[:, 2, t:t + 1],
                                  ALU.is_equal, ALU.mult)
                last.then_inc(s.picked, 1)

            def at(tab, i):
                return tab[:, bass.ds(i, 1), :, :].rearrange("p a f t -> p (a f) t")

            def gathered(s, i):
                copy(xg[:, 4:8, :], bank(7)[:, 0:4 * CAP].rearrange("p (c s) -> p c s", c=4))
                copy(spread[0:CAP, P:S], PS[0:CAP, 7, 4 * CAP:512]).then_inc(s.xg_by_vector, 1)

            def add_scattered(s, i):
                for t in range(TT):
                    for hf in range(2):
                        v.wait_ge(s.scattered, i * 4 + (2 * t + hf + 1))
                        o = x[:, t, hf * HALF:(hf + 1) * HALF]
                        tt(o, o, bank(6 + hf), ALU.add).then_inc(s.added, 1)

            def experts(s, mine, i, base):
                v.wait_ge(s.gathered, i * 2 + 2)
                gathered(s, i)
                choose(s, mine, now, at(table, i + (base + 1)), True)
                v.wait_ge(s.picked, i + 2)
                for j in range(GROUPS):
                    m = CAP * ffn_chunks(j)
                    v.wait_ge(s.silu_ready, i * GROUPS + (j + 1))
                    if j >= 2:
                        v.wait_ge(s.down_done, i * GROUPS + (j - 1))
                    tt(wk[2 + j % 2][:, 0:m], wk[j % 2][:, 0:m], bank(2 + j % 2)[:, 0:m],
                       ALU.mult).then_inc(s.hid_ready, 1)
                v.wait_ge(s.down_done, i * GROUPS + GROUPS)
                copy(wk[4][0:CAP, 0:HALF], PS[0:CAP, 4, :]).then_inc(s.y_by_vector, 1)
                add_scattered(s, i)

            def experts2(s, mine, i, base):
                v.wait_ge(s.gathered, i * 2 + 2)
                copy(cws[0:CAP, :], PS[0:CAP, 0, 4 * CAP:4 * CAP + 4])
                gathered(s, i)
                choose(s, mine, now2, at(table2, i + (base + 1)), False)
                v.wait_ge(s.picked, i + 2)

                def hidden(q):
                    v.wait_ge(s.silu_ready, i * 4 + (q + 1))
                    if q >= 2:
                        v.wait_ge(s.down_done, i * 4 + (q - 1))
                    tt(wk[2 + q % 2][:, 0:2 * CAP], wk[q % 2][:, 0:2 * CAP], bank(q % 2)[:, 2 * CAP:4 * CAP],
                       ALU.mult).then_inc(s.hid_ready, 1)

                def weigh(q):
                    y = PS[0:CAP, 2 + 2 * (q % 2):4 + 2 * (q % 2), :].rearrange("p b n -> p (b n)")
                    v.wait_ge(s.down_done, i * 4 + (q + 1))
                    if q == 0:
                        ins = ts(wk[4][0:CAP, :], y, cws[0:CAP, 0:1], None, ALU.mult)
                    else:
                        v.wait_ge(s.y_by_vector, i * 4 + q)
                        ins = stt(out=wk[4][0:CAP, :], in0=y, scalar=cws[0:CAP, q:q + 1], in1=wk[4][0:CAP, :],
                                  op0=ALU.mult, op1=ALU.add)
                    ins.then_inc(s.y_by_vector, 1)

                hidden(0)
                hidden(1)
                weigh(0)
                hidden(2)
                weigh(1)
                hidden(3)
                weigh(2)
                weigh(3)
                add_scattered(s, i)

            def sweeps(body, main, rest_s, tab, fields, weighted, n, k):
                def sweep(s, base, trips):
                    mine = Own(v, s.vstep)
                    nc.vector.memset(tick[:, 2:3], 0.0).then_inc(s.added, 1)
                    choose(s, mine, fields, tab[:, base, :, :], weighted)
                    with v.Fori(0, trips) as i:
                        with mine.loop(i, trips, 1):
                            body(s, mine, i, base)

                v.wait_ge(over_ready, k)
                sweep(main, 0, n)
                v.wait_ge(main.added, 4 * n + 1)
                more = v.value_load(over[0:1, k - 1:k], min_val=0, max_val=1)
                with v.If(more == 1):
                    sweep(rest_s, n, n * (PASSES - 1))
                    v.wait_ge(rest_s.added, 4 * n * (PASSES - 1) + 1)
                with v.Else():
                    v.nop()
                updated()

            norm(0)
            mixer(0)
            norm(1)
            dense()
            norm(2)
            mixer(1)
            norm(3)
            route()
            sweeps(experts, main1, rest1, table, now, True, EXPERTS, 1)
            norm(4, turned=False)
            v.wait_ge(norm_applied, 10)
            updated()
            norm(5)

            v.wait_ge(f_ready, 1)
            own.link(tt(lf[:], PS[:, 6, 0:16].rearrange("p (t e) -> p t e", t=TT),
                        bf[:].unsqueeze(1).to_broadcast([P, TT, HEADS]), ALU.add))
            own.link(ts(hs[:, 0:2, :], lf[:], -1.0, None, ALU.mult))
            tt(hs[:, 0:2, :], hs[:, 0:2, :], lf[:], ALU.max).then_inc(log_step, 1)
            v.wait_ge(h_turned, 20)
            for o in range(2):
                own.mark(nc.vector.memset(qz[64 * o:64 * o + 64, 1 - o::2, :], 0.0))
            v.wait_ge(log_step, LN_Z)
            stt(out=lf[:], in0=lf[:], scalar=0.0, in1=hs[:, 4:6, :], op0=ALU.min, op1=ALU.subtract).then_inc(log_step, 1)
            v.wait_ge(cum_ready, 1)
            own.mark(ts(c8[:].rearrange("p t e -> p (t e)"), PS[:, 7, 0:16], 8.0, None, ALU.mult))
            ts(negc[0:HEADS, :], PS[0:HEADS, 7, 128:384], -8.0, None, ALU.mult).then_inc(cum_copied, 1)
            r = [wk[2 + w].rearrange("p (c s) -> p c s", c=CH) for w in range(2)]
            v.wait_ge(qk_std, 1)
            own.link(nc.vector.reciprocal(wk[2], wk[2]))
            for o in range(2):
                a = slice(64 * o, 64 * o + 64)
                last = stt(out=qz[a, o::2, :], in0=chunks(0)[a], scalar=pcol[a, 36:37], in1=r[0][a],
                           op0=ALU.mult, op1=ALU.mult)
            last.then_inc(qk_hat, 1)
            v.wait_ge(qk_std, 2)
            own.link(nc.vector.reciprocal(wk[3], wk[3]))
            stt(out=uT[:], in0=chunks(2), scalar=pcol[:, 37:38], in1=r[1], op0=ALU.mult,
                op1=ALU.mult).then_inc(qk_hat, 1)
            v.wait_ge(proj2, 5)
            v.wait_ge(cbu_copied, 2)
            cu = wk[1].rearrange("p (c s) -> p c s", c=CH)
            tt(cpad[:, :, PAD:], chunks(2), cu, ALU.mult).then_inc(cc_used, 1)
            v.wait_ge(cc_used, 1)
            off = PAD - (TAPS2 - 1)
            acc = wk[2].rearrange("p (c s) -> p c s", c=CH)
            for k in range(TAPS2):
                for c in range(CH):
                    w = pcol[:, 24 + 4 * k + c:25 + 4 * k + c]
                    if k == 0:
                        own.mark(ts(acc[:, c, :], cpad[:, c, off:off + S], w, None, ALU.mult))
                    else:
                        own.settle(behind=CH - 1)
                        own.mark(stt(out=acc[:, c, :], in0=cpad[:, c, off + k:off + k + S], scalar=w,
                                     in1=acc[:, c, :], op0=ALU.mult, op1=ALU.add))
            own.settle()
            v.wait_ge(cbu_copied, 1)
            tt(yT[:, 4:8, :], acc, wk[0].rearrange("p (c s) -> p c s", c=CH), ALU.mult).then_inc(yconv, 1)
            for t in range(TT):
                L, n, each = (L1 if t else L0), P * (t + 1), 4 // (t + 1)
                v.wait_ge(att_logits, t + 1)
                for hd in range(HEADS):
                    o = PS[:, 2 + 2 * t + hd // each, (hd % each) * n:(hd % each + 1) * n]
                    own.mark(stt(out=L[:, hd, :], in0=o, scalar=c8[:, t, hd:hd + 1], in1=causal[:, S - n:S],
                                 op0=ALU.add, op1=ALU.add))
                own.settle()
                own.link(nc.vector.tensor_reduce(negmax[:, t, :], L, AX_X, ALU.max))
                ts(negmax[:, t, :], negmax[:, t, :], -0.125, None, ALU.mult).then_inc(att_max, 1)
            for t in range(TT):
                for b in range(1, 2 * (t + 1), 2):
                    v.wait_ge(att_turned, 2 * t + b + 1)
                    copy(PT[:, 4 * b:4 * b + 4, :],
                         bank(2 + 2 * t + b).rearrange("p (c s) -> p c s", c=4)).then_inc(att_pT_v, 1)
                v.wait_ge(att_exp, HEADS * (t + 1))
                own.link(nc.vector.reciprocal(rowsum[:, t, :], rowsum[:, t, :]))
                v.wait_ge(att_out, t + 1)
                tt(wk[2 + t][:, 0:512].rearrange("p (h n) -> p h n", h=HEADS),
                   bank(0).rearrange("p (h n) -> p h n", h=HEADS),
                   rowsum[:, t, :].unsqueeze(2).to_broadcast([P, HEADS, 64]), ALU.mult).then_inc(att_y, 1)
            for k in range(2):
                v.wait_ge(merge_mm, k + 1)
                own.mark(tt(sgu[:, k, :], sgu[:, k, :], bank(2 * k, 2), ALU.mult))
            for k in range(2):
                v.wait_ge(merge_mm, 3 + k)
                own.link(tt(sgu[:, 2 + k, :], sgu[:, 2 + k, :], bank(4 + 2 * k, 2), ALU.mult))
                tt(sgu[:, k, :], sgu[:, k, :], sgu[:, 2 + k, :], ALU.add).then_inc(merged, 1)
            add_rows(0, o_done, 3)
            norm(6)
            route2()
            sweeps(experts2, main2, rest2, table2, now2, False, GROUPS2, 2)
            norm(7)
            for t in range(TT):
                v.wait_ge(pw_done, t + 1)
                v.wait_ge(pg_act, t + 1)
                own.link(tt(wk[t], wk[t], bank(4 + 2 * t, 2), ALU.mult))
                tt(x[:, t, :], x[:, t, :], wk[t], ALU.add).then_inc(x_updated, 1)


def kernel(**inputs):
    import numpy as _np
    import concourse.bacc as _bacc
    from concourse import mybir as _mybir
    from concourse.bass_utils import run_bass_kernel_spmd as _run

    nc = _bacc.Bacc("TRN2", target_bir_lowering=False, num_devices=1)
    arrays, aps = {}, {}
    for name in INS:
        a = _np.ascontiguousarray(inputs[name])
        arrays[f"in_{name}_dram"] = a
        aps[name] = nc.dram_tensor(f"in_{name}_dram", a.shape, _mybir.dt.from_np(a.dtype), kind="ExternalInput").ap()
    out = nc.dram_tensor("out_dram", (1, S, D), _mybir.dt.float32, kind="ExternalOutput").ap()
    build(nc, aps, out)
    r = _run(nc, [arrays], core_ids=[0])
    return r.results[0]["out_dram"]
```

```python
from contextlib import ExitStack

import concourse.bass as bass
from concourse import mybir

F32 = mybir.dt.float32
F32R = mybir.dt.float32r
I32 = mybir.dt.int32
ALU = mybir.AluOpType
ACT = mybir.ActivationFunctionType
AX_X = mybir.AxisListType.X

P = 128
S = 256
TT = S // P
D = 1024
KC = D // P
EPS = 1e-6
HALF = 512
CH = 4
TAPS = 31
PAD = TAPS - 1
D_FF = 2816
FFC = D_FF // P
GROUPS = 6
EXPERTS = 8
HEADS = 8
TAPS2 = 3
DE = 256
GROUPS2 = 4
CAP = 96
PASSES = -(-S // CAP)
SLOTS = 6
TILE = 2048
SPLITS = 3
NEG = -1.0e30

INS = ["x", "norm_mix", "w_in", "conv_w", "conv_b", "conv_ng", "conv_nb", "sgu_ng", "sgu_nb", "sgu_w",
       "sgu_b", "w_out", "norm_ffn", "ffn_wg", "ffn_wu", "ffn_wd", "moe_router", "moe_wg", "moe_wu",
       "moe_wd", "norm_final", "p_2", "attn_norm_g_2", "w_in_2", "b_f_2", "q_norm_g_2", "k_norm_g_2",
       "conv_w_2", "w_out_att_2", "w_out_conv_2", "w_o_2", "ffn_norm_g_2", "w_rg_2", "b_rg_2", "w_re_2",
       "b_re_2", "w_gate_2", "w_up_2", "w_down_2", "ple_norm_g_2", "w_pg_2", "w_ple_2"]


class Own:

    def __init__(self, eng, sem):
        self.eng, self.sem, self.n = eng, sem, 0

    def mark(self, ins):
        ins.then_inc(self.sem, 1)
        self.n += 1

    def settle(self, behind=0):
        self.eng.wait_ge(self.sem, self.n - behind)

    def link(self, ins):
        self.mark(ins)
        self.settle()


class Freed:

    def __init__(self, sem, at, each=0):
        self.sem, self.at, self.each = sem, at, each

    def wait(self, eng, i=None):
        eng.wait_ge(self.sem, self.at if i is None else i * self.each + self.at)


class Stream:

    def __init__(self, landed, first_slot=0):
        self.landed, self.total = landed, [0] * SLOTS
        self.t, self.where, self.segments = first_slot, {}, []

    def segment(self, tiles, trips=1):
        per, t0 = [0] * SLOTS, self.t
        for j, (_, n, _, _) in enumerate(tiles):
            per[(t0 + j) % SLOTS] += 16 * n
        inside = [0] * SLOTS
        for j, (name, n, _, _) in enumerate(tiles):
            s = (t0 + j) % SLOTS
            inside[s] += 16 * n
            self.where[name] = (s, self.total[s] + inside[s], per[s])
        assert trips == 1 or len(tiles) % SLOTS == 0
        for s in range(SLOTS):
            self.total[s] += per[s] * trips
        self.t += len(tiles) * trips
        self.segments.append((t0, tiles, trips))

    def arrived(self, eng, name, i=None):
        s, at, each = self.where[name]
        eng.wait_ge(self.landed[s], at if i is None else i * each + at)
        return s


def build(nc, A, out):
    ctx = ExitStack()
    with ctx:
        def sb(name, shape, dt=F32):
            return ctx.enter_context(nc.sbuf_tensor(name, shape, dt))

        def sem(name):
            return ctx.enter_context(nc.semaphore(name))

        ring = sb("ring", [P, SLOTS, TILE])
        x = sb("x_res", [P, TT, D])
        h = sb("h", [P, TT, D])
        hT = sb("hT", [P, KC, S])
        yT = sb("yT", [P, KC, S])
        gain = sb("gain", [P, D])
        w_high = sb("w_high", [P, SPLITS, TILE], F32R)
        w_low = sb("w_low", [P, SPLITS, TILE], F32R)
        xg_high = sb("xg_high", [P, KC, CAP], F32R)
        xg_low = sb("xg_low", [P, KC, CAP], F32R)
        hg_high = sb("hg_high", [P, 4, CAP], F32R)
        hg_low = sb("hg_low", [P, 4, CAP], F32R)
        work = sb("work", [P, 5, D])
        wk = [work[:, i, :] for i in range(5)]
        cpad = sb("cpad", [P, CH, PAD + S])
        uT = sb("uT", [P, CH, S])
        vn = sb("vn", [P, TT, HALF])
        xg = uT[:].rearrange("p c s -> p (c s)")[:, 0:KC * CAP].rearrange("p (c s) -> p c s", c=KC)
        pick = sb("pick", [P, TT, CAP])
        pickg = sb("pickg", [P, TT, CAP])
        spread = sb("spread", [P, S])
        spread_next = vn[0:CAP, 0, 0:S]
        ident = sb("ident", [P, P])
        upper = sb("upper", [P, P])
        above = sb("above", [P, P])
        ones = sb("ones", [P, P])
        block64 = sb("block64", [P, P])
        causal = sb("causal", [P, S])
        tie = sb("tie", [P, EXPERTS, EXPERTS])
        head_row = sb("head_row", [P, HEADS, P])
        slot_i = sb("slot_i", [P, CAP], I32)
        slot_no = sb("slot_no", [P, CAP])
        sgu = sb("sgu", [P, 4, D])
        wsT = sgu[:, 0, :].rearrange("p (l h t) -> p l h t", l=2, h=4)
        sgb = sgu[:, 1, :].rearrange("p (l h t) -> p l h t", l=2, h=4)
        sng = sgu[:, 2, :].rearrange("p (l n) -> p l n", l=2)
        snb = sgu[:, 3, :].rearrange("p (l n) -> p l n", l=2)
        qz = h[:].rearrange("p t (a s) -> p (t a) s", s=S)
        L1 = hT[:]
        L0 = work[:, 4, :].rearrange("p (h k) -> p h k", h=HEADS)
        PT = work[:, 0:2, :].rearrange("p a (b s) -> p (a b) s", s=P)
        NROW = 38
        rows = work[0:NROW, 2, 0:P]
        rowsw = work[0:CH * TAPS, 2, P:3 * P].rearrange("p (l n) -> p l n", l=2)
        pcol = sb("pcol", [P, NROW])
        wcol = sb("wcol", [P, 2, CH * TAPS])
        router1 = sb("router1", [P, KC, EXPERTS])
        router2 = sb("router2", [P, KC, 20])
        wf = sb("wf", [P, KC, HEADS])
        bias2 = sb("bias2", [P, 20])
        bf = sb("bf", [P, HEADS])
        eps_c = sb("eps_c", [P, 1])
        half_c = sb("half_c", [P, 8])
        ms = sb("ms", [P, 8])
        rstd = sb("rstd", [P, 8])
        ss = sb("ss", [P, 2])
        s8 = sb("s8", [P, 8])
        lg = sb("lg", [P, TT, 20])
        shifted = sb("shifted", [P, TT, 20])
        ex = sb("ex", [P, TT, 20])
        mk = sb("mk", [P, TT, 20])
        cnt = sb("cnt", [P, TT, 20])
        mx = sb("mx", [P, 2 + 8])
        den = sb("den", [P, 2 + 8])
        pair_gt, pair_eq = (work[:, 3, k * P:(k + 1) * P] for k in range(2))
        ntab = (PASSES * EXPERTS) + 1
        table = sb("table", [P, ntab, 3, TT])
        table2 = sb("table2", [P, PASSES * GROUPS2 + 1, 6, TT])
        now = sb("now", [P, 3, TT])
        now2 = sb("now2", [P, 6, TT])
        cws = sb("cws", [P, 4])
        over_f = sb("over_f", [P, 2])
        over = sb("over", [1, 2], I32)
        ptok = work[:, 3, 0:TT * DE].rearrange("p (t d) -> p t d", t=TT)
        negmax = sb("negmax", [P, TT, HEADS])
        rowsum = sb("rowsum", [P, TT, HEADS])
        pT = sb("pT", [P, 2, S])
        c8 = sb("c8", [P, TT, HEADS])
        negc = spread[0:HEADS, :]
        lf = sb("lf", [P, TT, HEADS])
        hs = sb("hs", [P, 6, HEADS])
        tick = sb("tick", [1, 4])
        PS = ctx.enter_context(nc.psum_tensor("PS", [P, 8, HALF], F32))

        def bank(b, n=1):
            return PS[:, b:b + n, :].rearrange("p b n -> p (b n)")

        def chunks(b, n=2):
            return PS[:, b:b + n, :].rearrange("p b (c s) -> p (b c) s", s=S)

        x_landed = sem("x_landed")
        sgu_landed = sem("sgu_landed")
        rows_landed = sem("rows_landed")
        small_landed = sem("small_landed")
        gain_landed = sem("gain_landed")
        consts_made = sem("consts_made")
        consts_step = sem("consts_step")
        sgu_masked = sem("sgu_masked")
        params_turned = sem("params_turned")
        params_ready = sem("params_ready")
        landed = [sem(f"landed{s}") for s in range(SLOTS)]
        vstep = sem("vector_step")
        x_updated = sem("x_updated")
        sumsq_ready, ms_ready, rstd_ready = sem("sumsq_ready"), sem("ms_ready"), sem("rstd_ready")
        norm_applied, h_turned = sem("norm_applied"), sem("h_turned")
        hT_by_scalar, hT_by_vector = sem("hT_by_scalar"), sem("hT_by_vector")
        proj_done, gate_act, v_act, u_act = sem("proj_done"), sem("gate_act"), sem("v_act"), sem("u_act")
        conv_done, mean_done, centred, squared = sem("conv_done"), sem("mean_done"), sem("centred"), sem("squared")
        var_done, std_done, conv_hat, conv_act = sem("var_done"), sem("std_done"), sem("conv_hat"), sem("conv_act")
        v_centred, v_squared, v_ready = sem("v_centred"), sem("v_squared"), sem("v_ready")
        mixed, sgu_out, out_done = sem("mixed"), sem("sgu_out"), sem("out_done")
        gu_ready, silu_ready, hid_ready, down_done = (sem("ffn_gu_ready"), sem("ffn_silu_ready"),
                                                      sem("ffn_hid_ready"), sem("ffn_down_done"))
        logits_ready, mask_ready, rank_ready = sem("logits_ready"), sem("mask_ready"), sem("rank_ready")
        exps_wanted, exps_ready = sem("exps_wanted"), sem("exps_ready")
        over_ready = sem("over_ready")

        class Pass:

            def __init__(self, name):
                self.picked = sem(f"{name}_picked")
                self.gathered = sem(f"{name}_gathered")
                self.xg_by_scalar = sem(f"{name}_xg_by_scalar")
                self.xg_by_vector = sem(f"{name}_xg_by_vector")
                self.gu_ready = sem(f"{name}_gu_ready")
                self.silu_ready = sem(f"{name}_silu_ready")
                self.hid_ready = sem(f"{name}_hid_ready")
                self.down_done = sem(f"{name}_down_done")
                self.y_by_vector = sem(f"{name}_y_by_vector")
                self.scattered = sem(f"{name}_scattered")
                self.added = sem(f"{name}_added")

        class Pass1(Pass):

            def __init__(self, name):
                self.picked = sem(f"{name}_picked")
                self.gathered = sem(f"{name}_gathered")
                self.xg_high = sem(f"{name}_xg_high")
                self.xg_low = sem(f"{name}_xg_low")
                self.high_taken = sem(f"{name}_high_taken")
                self.low_taken = sem(f"{name}_low_taken")
                self.used = sem(f"{name}_tiles_used")
                self.silu_ready = sem(f"{name}_silu_ready")
                self.hid_ready = sem(f"{name}_hid_ready")
                self.turned = sem(f"{name}_hid_turned")
                self.hg_high = sem(f"{name}_hg_high")
                self.hg_low = sem(f"{name}_hg_low")
                self.y_ready = sem(f"{name}_y_ready")
                self.scattered = sem(f"{name}_scattered")
                self.added = sem(f"{name}_added")

        main1, rest1 = Pass1("moe"), Pass1("moe_rest")
        main2, rest2 = Pass("moe2"), Pass("moe2_rest")
        rest_landed = [[sem(f"rest{k}_landed{s}") for s in range(SLOTS)] for k in (1, 2)]

        proj2 = sem("proj2_done")
        f_ready, log_step, cum_ready, cum_copied = (
            sem(n) for n in ("f_ready", "log_step", "cum_ready", "cum_copied"))
        ABS_Z, EXP_Z, LN_Z, LOG_F = 1, 2, 3, 4
        qk_sq, qk_ms, qk_std, qk_hat = sem("qk_squared"), sem("qk_meansq"), sem("qk_std"), sem("qk_hat")
        v2_copied, cbu_copied, cc_used, yconv = (
            sem(n) for n in ("v2_copied", "cb_cu_copied", "cc_used", "yconv_ready"))
        gates_act = sem("gates_act")
        att_logits, att_shift, att_max, att_exp, att_turned, att_pT_s, att_pT_v, att_out, att_y, att_yturned, att_yT = (
            sem(n) for n in ("att_logits", "att_shifted", "att_max", "att_exp", "att_turned", "att_pT_scalar", "att_pT_vector",
                             "att_out", "att_y", "att_yturned", "att_yT"))
        merge_mm, merged, o_done = sem("merge_mm"), sem("merged"), sem("o_done")
        pw_done, pg_done, pg_act = (sem(n) for n in ("pw_done", "pg_done", "pg_act"))
        stored = sem("stored")

        def slot(s):
            return ring[:, s, :]

        def by8(s):
            return ring[:, s, :].rearrange("p (k n) -> p k n", k=KC)

        def by4(s):
            return ring[:, s, :].rearrange("p (k n) -> p k n", k=4)

        def by2(s):
            return ring[:, s, :].rearrange("p (k n) -> p k n", k=2)

        def split(part, k, chunks_):
            return part[:, k % SPLITS, :].rearrange("p (k n) -> p k n", k=chunks_)

        def cols(w, c0, n, k0=0, nk=KC):
            return w[k0 * P:(k0 + nk) * P, c0:c0 + n].rearrange("(k p) n -> p k n", p=P)

        def kays(w, k0, n):
            return w[k0 * P:(k0 + n) * P, :].rearrange("(k p) n -> p k n", p=P)

        def expert(w, i):
            if isinstance(i, int):
                return w[i]
            return w[bass.ds(i, 1), :, :].rearrange("a r c -> (a r) c")

        stream = Stream(landed)

        def fixed(name, s_view, src, freed):
            return (name, 1, lambda i, s: [(s_view(s), src)], freed)

        def column_tiles(name, w, c0, freed):
            return [fixed((name, kh), by4, cols(w, c0, 512, 4 * kh, 4), freed) for kh in range(2)]

        def row_tiles(name, w, k0, n, signal, at):
            return [fixed((name, m), by2, kays(w, k0 + 2 * m, 2), Freed(signal, at + 2 * m + 2)) for m in range(n // 2)]

        def mixer_tiles(l):
            w, wo = A["w_in"][l], A["w_out"][l]
            return (column_tiles((l, "gate"), w, 512, Freed(proj_done, 4 * l + 1))
                    + column_tiles((l, "a"), w, 0, Freed(proj_done, 4 * l + 2))
                    + column_tiles((l, "v"), w, 1536, Freed(proj_done, 4 * l + 3))
                    + column_tiles((l, "u"), w, 1024, Freed(proj_done, 4 * l + 4))
                    + row_tiles((l, "out_sgu"), wo, 4, 4, out_done, 8 * l)
                    + row_tiles((l, "out_conv"), wo, 0, 4, out_done, 8 * l + 4))

        def ffn_chunks(j):
            return min(4, FFC - 4 * j)

        HALVES = FFC // 2

        def dense_tiles():
            def one(kind, j):
                if kind == "d":
                    return fixed(("ffn", kind, j), by2, kays(A["ffn_wd"][0], 2 * j, 2), Freed(down_done, j + 1))
                return fixed(("ffn", kind, j), by8, cols(A["ffn_w" + kind][0], 256 * j, 256), Freed(gu_ready, j + 1))

            tiles = []
            for j in range(HALVES):
                tiles += [one("g", j), one("u", j)]
                if j:
                    tiles.append(one("d", j - 1))
            return tiles + [one("d", HALVES - 1)]

        order = []
        for j in range(GROUPS):
            parts = 2 if ffn_chunks(j) == 4 else 1
            order += [("g", j, m) for m in range(parts)] + [("u", j, m) for m in range(parts)]
            if j:
                order += [("d", j - 1, m) for m in range(2)]
        order.append(("d", GROUPS - 1, 0))
        TILES1 = len(order)
        TURN1 = -(-TILES1 // SLOTS) * SLOTS
        assert TURN1 % SPLITS == 0 and TURN1 - TILES1 == SPLITS
        number = {t: k for k, t in enumerate(order)}
        up_end = [number[("u", j, 1 if ffn_chunks(j) == 4 else 0)] for j in range(GROUPS)]
        down_end = [number[("d", j, 1 if ffn_chunks(j) == 4 else 0)] for j in range(GROUPS)]
        turn_at = [number[("u", j + 1, 0)] - 1 for j in range(GROUPS - 1)] + [down_end[GROUPS - 2]]

        def moe_tiles(s):
            def one(k):
                kind, j, m = order[k]

                def load(i, slot_):
                    if kind == "d":
                        w = expert(A["moe_wd"][0], i)
                        if (j, m) == (0, 0):
                            return [(by2(slot_)[:, c:c + 1, :], kays(w, c, 1)) for c in (1, 0)]
                        return [(by2(slot_), kays(w, 4 * j + 2 * m, 2))]
                    w = expert(A["moe_w" + kind][0], i)
                    if ffn_chunks(j) == 4:
                        return [(by4(slot_), cols(w, 512 * j, 512, 4 * m, 4))]
                    return [(by8(slot_), cols(w, 512 * j, 256))]
                return (("moe", k), 2 if order[k] == ("d", 0, 0) else 1, load, Freed(s.low_taken, k + 1, TILES1))

            tiles = [one(k) for k in range(TILES1)]
            return tiles + [(("hole", m), 0, None, tiles[TILES1 + m - SLOTS][3]) for m in range(TURN1 - TILES1)]

        def moe2_tiles(s):
            def one(kind, q, freed):
                name = {"g": "w_gate_2", "u": "w_up_2", "d": "w_down_2"}[kind]

                def load(i, slot_):
                    view = by2(slot_) if kind == "d" else by8(slot_)
                    return [(view, expert(A[name][0], i * 4 + q).rearrange("(k p) n -> p k n", p=P))]
                return (("moe2", kind, q), 1, load, freed)

            tiles = []
            for q in range(4):
                tiles += [one("g", q, Freed(s.gu_ready, q + 1, 4)), one("u", q, Freed(s.gu_ready, q + 1, 4))]
                if q:
                    tiles.append(one("d", q - 1, Freed(s.down_done, q, 4)))
            return tiles + [one("d", 3, Freed(s.down_done, 4, 4))]

        stream.segment(mixer_tiles(0))
        stream.segment(dense_tiles())
        stream.segment(mixer_tiles(1))
        stream.segment(moe_tiles(main1), EXPERTS)
        w2 = A["w_in_2"][0]
        two = [("q", 0), ("k", 512), ("v", 1024), ("cb", 1544), ("cc", 2056), ("cu", 2568),
               ("ga0", 3080), ("ga1", 3592), ("gb0", 4104), ("gb1", 4616)]
        stream.segment([t for k, (n, c) in enumerate(two) for t in column_tiles(n, w2, c, Freed(proj2, k + 1))]
                       + [fixed(("out_att", m), by2, kays(A["w_out_att_2"][0], 2 * m, 2), Freed(merge_mm, 2))
                          for m in range(2)]
                       + [fixed(("out_conv2", m), by2, kays(A["w_out_conv_2"][0], 2 * m, 2), Freed(merge_mm, 4))
                          for m in range(2)]
                       + row_tiles("o", A["w_o_2"][0], 0, 8, o_done, 0))
        stream.segment(moe2_tiles(main2), GROUPS2)
        stream.segment(row_tiles("ple", A["w_ple_2"][0], 0, 2, pw_done, 0)
                       + row_tiles("pg", A["w_pg_2"][0], 0, 8, pg_done, 0))

        restream1 = Stream(rest_landed[0])
        restream1.segment(moe_tiles(rest1), EXPERTS * (PASSES - 1))
        restream2 = Stream(rest_landed[1])
        restream2.segment(moe2_tiles(rest2), GROUPS2 * (PASSES - 1))

        block = ctx.enter_context(nc.Block())

        @block.sync
        def _(sp):
            for t in range(TT):
                sp.dma_start(x[:, t, :], A["x"][0, t * P:(t + 1) * P, :]).then_inc(x_landed, 16)
            sp.wait_ge(rows_landed, 16 * 10)
            sp.wait_ge(small_landed, 16 * 14)

            def load(st, s, tile, i, at):
                for dst, src in tile[2](i, s):
                    sp.dma_start(dst, src).then_inc(st.landed[s], 16)

            def turn_of(st, t0, tiles, j, turn, before=None):
                n = len(tiles)
                if tiles[j % n][1]:
                    tiles[(j - SLOTS) % n][3].wait(sp, before if before is not None else turn)
                    load(st, (t0 + j) % SLOTS, tiles[j % n], turn, j)

            def straight(st, k):
                t0, tiles, trips = st.segments[k]
                n = len(tiles)
                if k:
                    _, before, turns = st.segments[k - 1]
                first = tiles if trips == 1 else tiles[:SLOTS]
                for j, tile in enumerate(first):
                    if j >= SLOTS:
                        tiles[j - SLOTS][3].wait(sp)
                    elif k:
                        prev = before[len(before) - SLOTS + j]
                        prev[3].wait(sp, turns - 1 if turns > 1 else None)
                    load(st, (t0 + j) % SLOTS, tile, 0, j)

            def looped(st, k):
                t0, tiles, trips = st.segments[k]
                n = len(tiles)
                with sp.Fori(0, trips - 1) as i:
                    for j in range(SLOTS, n):
                        turn_of(st, t0, tiles, j, i)
                    for j in range(SLOTS):
                        turn_of(st, t0, tiles, j, i + 1, i)
                for j in range(SLOTS, n):
                    turn_of(st, t0, tiles, j, trips - 1)

            def rest(st, passes_of, n_over, main_freed, rest_freed):
                sp.wait_ge(over_ready, n_over)
                more = sp.value_load(over[0:1, n_over - 1:n_over], min_val=0, max_val=1)
                with sp.If(more == 1):
                    main_freed.wait(sp)
                    t0, tiles, trips = st.segments[0]
                    n = len(tiles)
                    for j in range(SLOTS):
                        load(st, j, tiles[j], 0, j)
                    for j in range(SLOTS, n):
                        turn_of(st, 0, tiles, j, 0)
                    for r in range(PASSES - 1):
                        with sp.Fori(0 if r else 1, passes_of) as e:
                            for j in range(n):
                                if tiles[j][1]:
                                    turn = e + (r * passes_of if j >= SLOTS else r * passes_of - 1)
                                    tiles[(j - SLOTS) % n][3].wait(sp, turn)
                                    load(st, j % SLOTS, tiles[j], e, j)
                    rest_freed.wait(sp)
                with sp.Else():
                    sp.nop()
                sp.nop()

            for k in (0, 1, 2, 3):
                straight(stream, k)
            looped(stream, 3)
            rest(restream1, EXPERTS, 1, Freed(main1.low_taken, EXPERTS * TILES1),
                 Freed(rest1.low_taken, EXPERTS * TILES1 * (PASSES - 1)))
            straight(stream, 4)
            straight(stream, 5)
            looped(stream, 5)
            rest(restream2, GROUPS2, 2, Freed(main2.down_done, 4 * GROUPS2),
                 Freed(rest2.down_done, 4 * GROUPS2 * (PASSES - 1)))
            straight(stream, 6)
            for t in range(TT):
                sp.wait_ge(x_updated, 14 + t + 1)
                sp.dma_start(out[0, t * P:(t + 1) * P, :], x[:, t, :]).then_inc(stored, 16)
            sp.wait_ge(stored, 16 * TT)

        @block.gpsimd
        def _(pool):
            n = [0]

            def link(ins):
                ins.then_inc(consts_step, 1)
                n[0] += 1
                pool.wait_ge(consts_step, n[0])

            def row_gain(k):
                names = [("norm_mix", 0), ("norm_ffn", 0), ("norm_mix", 1), ("norm_ffn", 1), ("norm_final", None),
                         ("attn_norm_g_2", 0), ("ffn_norm_g_2", 0), ("ple_norm_g_2", 0)]
                name, l = names[k]
                g = A[name] if l is None else A[name][l]
                return g.rearrange("(a d) -> a d", a=1).broadcast_to([P, D])

            pool.dma_start(gain[:], row_gain(0)).then_inc(gain_landed, 16)
            link(nc.gpsimd.memset(ident[:], 0.0))
            link(nc.gpsimd.affine_select(out=ident[:], in_=ident[:], compare_op=ALU.not_equal, fill=1.0, base=0,
                                         pattern=[[-1, P]], channel_multiplier=1))
            link(nc.gpsimd.memset(half_c[:], -0.5))
            link(nc.gpsimd.memset(eps_c[:], EPS))
            link(nc.gpsimd.memset(cpad[:], 0.0))
            link(nc.gpsimd.memset(block64[:], 0.0))
            link(nc.gpsimd.memset(block64[0:64, 0:64], 1.0 / 64))
            link(nc.gpsimd.memset(block64[64:128, 64:128], 1.0 / 64))
            pool.wait_ge(sgu_landed, 32)
            for l in range(2):
                w = wk[l][:, 0:512].rearrange("p (h s) -> p h s", h=4)
                nc.gpsimd.affine_select(out=w, in_=w, compare_op=ALU.is_ge, fill=0.0, base=0,
                                        pattern=[[0, 4], [-1, P]], channel_multiplier=1).then_inc(sgu_masked, 1)
            link(nc.gpsimd.memset(ones[:], 1.0))
            link(nc.gpsimd.affine_select(out=upper[:], in_=ones[:], compare_op=ALU.is_ge, fill=0.0, base=0,
                                         pattern=[[1, P]], channel_multiplier=-1))
            link(nc.gpsimd.affine_select(out=above[:], in_=ones[:], compare_op=ALU.is_ge, fill=0.0, base=-1,
                                         pattern=[[1, P]], channel_multiplier=-1))
            link(nc.gpsimd.memset(causal[:], 0.0))
            link(nc.gpsimd.affine_select(out=causal[:, P:], in_=causal[:, P:], compare_op=ALU.is_ge, fill=NEG, base=0,
                                         pattern=[[-1, P]], channel_multiplier=1))
            link(nc.gpsimd.memset(tie[:], 1.0))
            link(nc.gpsimd.affine_select(out=tie[:], in_=tie[:], compare_op=ALU.is_ge, fill=0.0, base=-1,
                                         pattern=[[1, EXPERTS], [-1, EXPERTS]], channel_multiplier=0))
            link(nc.gpsimd.memset(head_row[:], 1.0))
            link(nc.gpsimd.affine_select(out=head_row[:], in_=head_row[:], compare_op=ALU.is_equal, fill=0.0, base=0,
                                         pattern=[[-1, HEADS], [0, P]], channel_multiplier=1))
            link(nc.gpsimd.iota(slot_i[:], pattern=[[1, CAP]], base=0, channel_multiplier=0))
            link(nc.gpsimd.tensor_copy(slot_no[:], slot_i[:]))
            link(nc.gpsimd.memset(table[:], 0.0))
            nc.gpsimd.memset(table2[:], 0.0).then_inc(consts_made, 1)
            asks = ["norm", "sgu", "norm", "norm", "sgu", "norm", "norm", "norm", "norm", "norm"]
            norm = 0
            for k, kind in enumerate(asks):
                m = 8 if kind == "sgu" else 2
                pool.wait_ge(ms_ready, k + 1)
                nc.gpsimd.tensor_tensor(rstd[:, 0:m], ms[:, 0:m], half_c[:, 0:m], ALU.pow).then_inc(rstd_ready, 1)
                if kind == "norm":
                    norm += 1
                    if norm < 8:
                        pool.wait_ge(norm_applied, 2 * norm)
                        pool.dma_start(gain[:], row_gain(norm)).then_inc(gain_landed, 16)

        @block.scalar
        def _(act):
            for l in range(2):
                act.dma_start(wk[l][:, 0:512].rearrange("p (h s) -> p h s", h=4),
                              A["sgu_w"][l].rearrange("h t s -> t h s")).then_inc(sgu_landed, 16)
            r = 0
            for name in ("conv_b", "conv_ng", "conv_nb"):
                act.dma_start(rows[r:r + 8, :], A[name].rearrange("l (c p) -> (l c) p", p=P)).then_inc(rows_landed, 16)
                r += 8
            act.dma_start(rows[r:r + 12, :],
                          A["conv_w_2"][0].rearrange("w (c p) -> (w c) p", p=P)).then_inc(rows_landed, 16)
            r += 12
            for name in ("q_norm_g_2", "k_norm_g_2"):
                for half in range(2):
                    act.dma_start(rows[r:r + 1, 64 * half:64 * half + 64], A[name]).then_inc(rows_landed, 16)
                r += 1
            for l in range(2):
                act.dma_start(rowsw[:, l, :],
                              A["conv_w"][l].rearrange("w a (c p) -> (w a c) p", p=P)).then_inc(rows_landed, 16)
            for l in range(2):
                act.dma_start(sgb[:, l].rearrange("p h t -> p (h t)"),
                              A["sgu_b"][l:l + 1].rearrange("a h t -> a (h t)").broadcast_to([P, 512])
                              ).then_inc(small_landed, 16)
                act.dma_start(sng[:, l, :], A["sgu_ng"][l:l + 1, :].broadcast_to([P, HALF])).then_inc(small_landed, 16)
                act.dma_start(snb[:, l, :], A["sgu_nb"][l:l + 1, :].broadcast_to([P, HALF])).then_inc(small_landed, 16)
            act.dma_start(router1[:], A["moe_router"][0].rearrange("(k p) n -> p k n", p=P)).then_inc(small_landed, 16)
            act.dma_start(router2[:, :, 0:4], A["w_rg_2"][0].rearrange("(k p) n -> p k n", p=P)).then_inc(small_landed, 16)
            act.dma_start(router2[:, :, 4:20], A["w_re_2"][0].rearrange("(k p) n -> p k n", p=P)).then_inc(small_landed, 16)
            act.dma_start(wf[:], cols(w2, 1536, HEADS)).then_inc(small_landed, 16)
            act.dma_start(bias2[:, 0:4], A["b_rg_2"].broadcast_to([P, 4])).then_inc(small_landed, 16)
            act.dma_start(bias2[:, 4:20], A["b_re_2"].broadcast_to([P, 16])).then_inc(small_landed, 16)
            act.dma_start(bf[:], A["b_f_2"].broadcast_to([P, HEADS])).then_inc(small_landed, 16)
            act.dma_start(ptok[:], A["p_2"][0, 0].rearrange("(t p) d -> p t d", p=P)).then_inc(small_landed, 16)

            def norm(n, turn=True):
                if n == 0:
                    act.wait_ge(x_landed, 32)
                else:
                    act.wait_ge(x_updated, 2 * n - 1)
                act.activation(h[:, 0, :], x[:, 0, :], ACT.Square, accum_out=ss[:, 0:1]).then_inc(sumsq_ready, 1)
                if turn:
                    k = n if n < 4 else n - 1
                    for t in range(TT):
                        act.wait_ge(h_turned, 4 * k + 2 * t + 1)
                        act.activation(hT[:, 0:4, t * P:(t + 1) * P],
                                       bank(2 * t).rearrange("p (c s) -> p c s", c=4),
                                       ACT.Copy).then_inc(hT_by_scalar, 1)

            def mixer(l):
                act.wait_ge(proj_done, 4 * l + 1)
                act.activation(wk[0][:], bank(0, 2), ACT.Sigmoid).then_inc(gate_act, 1)
                act.wait_ge(proj_done, 4 * l + 3)
                act.activation(vn[:].rearrange("p t n -> p (t n)"), bank(4, 2), ACT.Gelu).then_inc(v_act, 1)
                act.wait_ge(proj_done, 4 * l + 4)
                act.activation(uT[:].rearrange("p c s -> p (c s)"), bank(6, 2), ACT.Gelu).then_inc(u_act, 1)
                act.wait_ge(v_centred, l + 1)
                act.activation(wk[3][:], vn[:].rearrange("p t n -> p (t n)"), ACT.Square).then_inc(v_squared, 1)
                act.wait_ge(centred, l + 1)
                act.activation(wk[2][:], wk[1][:], ACT.Square).then_inc(squared, 1)
                act.wait_ge(var_done, l + 1)
                act.activation(wk[2][:], bank(2, 2), ACT.Sqrt, bias=eps_c[:, 0:1]).then_inc(std_done, 1)
                act.wait_ge(params_ready, 2)
                for c in range(CH):
                    act.wait_ge(conv_hat, 2 * l + 1 + c // 2)
                    act.activation(yT[:, c, :], wk[1][:, c * S:(c + 1) * S], ACT.Silu,
                                   bias=pcol[:, 16 + 4 * l + c:17 + 4 * l + c],
                                   scale=pcol[:, 8 + 4 * l + c:9 + 4 * l + c]).then_inc(conv_act, 1)

            def high(st, s, i, k, wait=True):
                w = st.arrived(act, ("moe", k), i)
                if wait:
                    act.wait_ge(s.used, i * TILES1 + (k - SPLITS + 1))
                act.activation(w_high[:, k % SPLITS, :], slot(w), ACT.Copy).then_inc(s.high_taken, 1)

            def silu(s, i, j):
                m = P * ffn_chunks(j)
                act.wait_ge(s.used, i * TILES1 + (up_end[j] + 1))
                act.activation(wk[j % 2][0:CAP, 0:m], PS[0:CAP, j % 2, 0:m], ACT.Silu).then_inc(s.silu_ready, 1)

            def hidden_high(s, i, j):
                m = ffn_chunks(j)
                act.wait_ge(s.turned, i * GROUPS + (j + 1))
                act.activation(hg_high[:, 0:m, :], bank(6 + j % 2)[:, 0:m * CAP].rearrange("p (c s) -> p c s", c=m),
                               ACT.Copy).then_inc(s.hg_high, 1)

            def tokens_high(s, i):
                for b in range(2):
                    act.wait_ge(s.gathered, i * 2 + (b + 1))
                    act.activation(xg_high[:, 4 * b:4 * b + 4, :],
                                   bank(6 + b)[:, 0:4 * CAP].rearrange("p (c s) -> p c s", c=4),
                                   ACT.Copy).then_inc(s.xg_high, 1)

            def experts(st, s, i, last):
                for k in range(SPLITS, TILES1 + SPLITS):
                    if k < TILES1:
                        high(st, s, i, k)
                    elif not last:
                        high(st, s, i + 1, k - TILES1)
                    for j in range(GROUPS):
                        if k == up_end[j] + SPLITS:
                            silu(s, i, j)
                        if k == turn_at[j] + SPLITS:
                            hidden_high(s, i, j)
                    if k == turn_at[-1] + SPLITS and not last:
                        tokens_high(s, i + 1)
                act.wait_ge(s.used, i * TILES1 + TILES1)
                act.activation(wk[4][0:CAP, :], PS[0:CAP, 4:6, :].rearrange("p b n -> p (b n)"),
                               ACT.Copy).then_inc(s.y_ready, 1)

            def sweep1(st, s, n):
                for k in range(SPLITS):
                    high(st, s, 0, k, wait=False)
                tokens_high(s, 0)
                with act.Fori(0, n - 1) as i:
                    experts(st, s, i, False)
                experts(st, s, n - 1, True)

            def experts2(s, i):
                act.wait_ge(s.gathered, 2 * i + 1)
                act.activation(xg[:, 0:4, :], bank(6)[:, 0:4 * CAP].rearrange("p (c s) -> p c s", c=4), ACT.Copy)
                act.activation(spread[0:CAP, 0:P], PS[0:CAP, 6, 4 * CAP:512], ACT.Copy).then_inc(s.xg_by_scalar, 1)
                for q in range(4):
                    act.wait_ge(s.gu_ready, i * 4 + (q + 1))
                    if q >= 2:
                        act.wait_ge(s.hid_ready, i * 4 + (q - 1))
                    act.activation(wk[q % 2][:, 0:2 * CAP], bank(q % 2)[:, 0:2 * CAP], ACT.Silu).then_inc(s.silu_ready, 1)

            def route_exps(k, n):
                act.wait_ge(exps_wanted, k)
                act.activation(ex[:, :, 0:n], shifted[:, :, 0:n], ACT.Exp).then_inc(exps_ready, 1)

            act.wait_ge(params_turned, 1)
            act.activation(pcol[:], bank(0)[:, 0:NROW], ACT.Copy)
            act.activation(wcol[:].rearrange("p l w -> p (l w)"), bank(0)[:, NROW:NROW + 2 * CH * TAPS],
                           ACT.Copy).then_inc(params_ready, 1)
            act.wait_ge(params_turned, 2)
            act.activation(wsT[:].rearrange("p l h t -> p (l h t)"), bank(2, 2), ACT.Copy).then_inc(params_ready, 1)
            act.wait_ge(params_turned, 3)
            act.activation(pT[:].rearrange("p k s -> p (k s)"), bank(4), ACT.Copy).then_inc(params_ready, 1)
            norm(0)
            mixer(0)
            norm(1)
            for j in range(HALVES):
                act.wait_ge(gu_ready, j + 1)
                if j >= 2:
                    act.wait_ge(hid_ready, j - 1)
                act.activation(wk[j % 2][:, 0:512], bank(j % 2), ACT.Silu).then_inc(silu_ready, 1)
            norm(2)
            mixer(1)
            norm(3)
            route_exps(1, EXPERTS)
            sweep1(stream, main1, EXPERTS)
            act.wait_ge(over_ready, 1)
            more = act.value_load(over[0:1, 0:1], min_val=0, max_val=1)
            with act.If(more == 1):
                sweep1(restream1, rest1, EXPERTS * (PASSES - 1))
            with act.Else():
                act.nop()
            act.nop()
            norm(4, turn=False)
            norm(5)

            act.wait_ge(log_step, ABS_Z)
            act.activation(hs[:, 2:4, :], hs[:, 0:2, :], ACT.Exp, scale=-1.0).then_inc(log_step, 1)
            act.wait_ge(log_step, EXP_Z)
            act.activation(hs[:, 4:6, :], hs[:, 2:4, :], ACT.Ln, bias=ones[:, 0:1]).then_inc(log_step, 1)
            for k in range(2):
                act.wait_ge(proj2, k + 1)
                act.activation(wk[k][:], bank(2 * k, 2), ACT.Square).then_inc(qk_sq, 1)
            act.wait_ge(proj2, 3)
            act.activation(vn[:].rearrange("p t n -> p (t n)"), bank(4, 2), ACT.Copy).then_inc(v2_copied, 1)
            for k in range(2):
                act.wait_ge(qk_ms, k + 1)
                act.activation(wk[2 + k][:], bank(6, 2), ACT.Sqrt, bias=eps_c[:, 0:1]).then_inc(qk_std, 1)
            act.wait_ge(qk_hat, 2)
            act.wait_ge(proj2, 4)
            act.activation(wk[0][:], bank(0, 2), ACT.Copy).then_inc(cbu_copied, 1)
            act.wait_ge(proj2, 6)
            act.activation(wk[1][:], bank(4, 2), ACT.Copy).then_inc(cbu_copied, 1)
            for k, (dst, b) in enumerate(((sgu[:, 0], 0), (sgu[:, 1], 6), (sgu[:, 2], 4), (sgu[:, 3], 0))):
                act.wait_ge(proj2, 7 + k)
                act.activation(dst, bank(b, 2), ACT.Sigmoid).then_inc(gates_act, 1)
            for t in range(TT):
                L = L1 if t else L0
                act.wait_ge(att_max, t + 1)
                for hd in range(HEADS):
                    act.activation(L[:, hd, :], L[:, hd, :], ACT.Exp, bias=negmax[:, t, hd:hd + 1], scale=0.125,
                                   accum_out=rowsum[:, t, hd:hd + 1]).then_inc(att_exp, 1)
                for b in range(0, 2 * (t + 1), 2):
                    act.wait_ge(att_turned, 2 * t + b + 1)
                    act.activation(PT[:, 4 * b:4 * b + 4, :], bank(2 + 2 * t + b).rearrange("p (c s) -> p c s", c=4),
                                   ACT.Copy).then_inc(att_pT_s, 1)
                act.wait_ge(att_yturned, t + 1)
                act.activation(yT[:, 0:4, t * P:(t + 1) * P], bank(1).rearrange("p (c s) -> p c s", c=4),
                               ACT.Copy).then_inc(att_yT, 1)
            norm(6)
            route_exps(2, 20)
            with act.Fori(0, GROUPS2) as i:
                experts2(main2, i)
            act.wait_ge(over_ready, 2)
            more = act.value_load(over[0:1, 1:2], min_val=0, max_val=1)
            with act.If(more == 1):
                with act.Fori(0, GROUPS2 * (PASSES - 1)) as i:
                    experts2(rest2, i)
            with act.Else():
                act.nop()
            act.nop()
            norm(7)
            for t in range(TT):
                act.wait_ge(pg_done, 7 + t)
                act.activation(wk[t], bank(2 * t, 2), ACT.Sigmoid).then_inc(pg_act, 1)

        @block.tensor
        def _(pe):
            mm = nc.tensor.matmul

            def turn(n):
                for t in range(TT):
                    pe.wait_ge(norm_applied, 2 * n + t + 1)
                    for b in range(2):
                        for c in range(4):
                            last = nc.tensor.transpose(PS[:, 2 * t + b, c * P:(c + 1) * P],
                                                       h[:, t, (4 * b + c) * P:(4 * b + c + 1) * P], ident[:])
                        last.then_inc(h_turned, 1)

            def have_hT(n):
                k = n if n < 4 else n - 1
                pe.wait_ge(hT_by_scalar, 2 * k + 2)
                pe.wait_ge(hT_by_vector, 2 * k + 2)

            def landed_pair(name):
                return [stream.arrived(pe, (name, kh)) for kh in range(2)]

            def project_T(pair, b):
                for c in range(4):
                    for k in range(KC):
                        last = mm(chunks(b)[:, c, :], by4(pair[k // 4])[:, k % 4, c * P:(c + 1) * P], hT[:, k, :],
                                  start=(k == 0), stop=(k == KC - 1))
                return last

            def project(pair, b):
                for t in range(TT):
                    for k in range(KC):
                        last = mm(bank(b + t), hT[:, k, t * P:(t + 1) * P], by4(pair[k // 4])[:, k % 4, :],
                                  start=(k == 0), stop=(k == KC - 1))
                return last

            def rows_of_model(name, lhs, b, first, last_one, signal, n, ready=None):
                for m in range(n // 2):
                    s = stream.arrived(pe, (name, m))
                    if ready:
                        ready(m)
                    for t in range(TT):
                        for hf in range(2):
                            for k in range(2):
                                last = mm(bank(b + 2 * t + hf), lhs(2 * m + k)[:, t * P:(t + 1) * P],
                                          by2(s)[:, k, hf * HALF:(hf + 1) * HALF],
                                          start=(first and m == 0 and k == 0),
                                          stop=(last_one and m == n // 2 - 1 and k == 1))
                        last.then_inc(signal, 1)

            def mixer(l):
                have_hT(2 * l)
                project_T(landed_pair((l, "gate")), 0).then_inc(proj_done, 1)
                project_T(landed_pair((l, "a")), 2).then_inc(proj_done, 1)
                project(landed_pair((l, "v")), 4).then_inc(proj_done, 1)
                project_T(landed_pair((l, "u")), 6).then_inc(proj_done, 1)
                pe.wait_ge(v_ready, l + 1)
                for hd in range(4):
                    for n in range(TT):
                        last = mm(chunks(4)[:, hd, n * P:(n + 1) * P], vn[:, n, hd * P:(hd + 1) * P], wsT[:, l, hd, :],
                                  start=True, stop=True)
                last.then_inc(mixed, 1)
                pe.wait_ge(sgu_out, l + 1)
                rows_of_model((l, "out_sgu"), lambda k: yT[:, 4 + k, :], 4, True, False, out_done, 4)
                pe.wait_ge(conv_done, l + 1)
                for b in range(2):
                    last = mm(bank(b), block64[:], wk[1][:, b * HALF:(b + 1) * HALF], start=True, stop=True)
                last.then_inc(mean_done, 1)
                pe.wait_ge(squared, l + 1)
                for b in range(2):
                    last = mm(bank(2 + b), block64[:], wk[2][:, b * HALF:(b + 1) * HALF], start=True, stop=True)
                last.then_inc(var_done, 1)
                rows_of_model((l, "out_conv"), lambda k: yT[:, k, :], 4, False, True, out_done, 4,
                              ready=lambda m: pe.wait_ge(conv_act, 4 * l + 2 * (m + 1)))

            def dense():
                have_hT(1)

                def gate_up(j):
                    if j >= 2:
                        pe.wait_ge(hid_ready, j - 1)
                    for b, kind in ((j % 2, "g"), (2 + j % 2, "u")):
                        s = stream.arrived(pe, ("ffn", kind, j))
                        for c in range(2):
                            for k in range(KC):
                                last = mm(chunks(b, 1)[:, c, :], by8(s)[:, k, c * P:(c + 1) * P], hT[:, k, :],
                                          start=(k == 0), stop=(k == KC - 1))
                    last.then_inc(gu_ready, 1)

                def down(j):
                    pe.wait_ge(hid_ready, j + 1)
                    s = stream.arrived(pe, ("ffn", "d", j))
                    for t in range(TT):
                        for hf in range(2):
                            for c in range(2):
                                last = mm(bank(4 + 2 * t + hf), wk[2 + j % 2][:, c * S + t * P:c * S + (t + 1) * P],
                                          by2(s)[:, c, hf * HALF:(hf + 1) * HALF],
                                          start=(j == 0 and c == 0), stop=(j == HALVES - 1 and c == 1))
                    last.then_inc(down_done, 1)

                gate_up(0)
                for j in range(1, HALVES):
                    gate_up(j)
                    down(j - 1)
                down(HALVES - 1)

            def route(n, weights, ne, groups, k):
                have_hT(n)
                if k == 1:
                    pe.wait_ge(small_landed, 16 * 14)
                for t in range(TT):
                    for c in range(KC):
                        last = mm(PS[:, 0, t * ne:(t + 1) * ne], hT[:, c, t * P:(t + 1) * P], weights[:, c, :],
                                  start=(c == 0), stop=(c == KC - 1))
                last.then_inc(logits_ready, 1)
                pe.wait_ge(mask_ready, k)
                m = [mk[:, t, 0:groups] for t in range(TT)]
                mm(PS[:, 1, 0:groups], above[:], m[0], start=True, stop=True)
                mm(PS[:, 1, groups:2 * groups], ones[:], m[0], start=True, stop=False)
                mm(PS[:, 1, groups:2 * groups], above[:], m[1], start=False, stop=True)
                mm(PS[:, 1, 2 * groups:3 * groups], ones[:], m[0], start=True, stop=False)
                mm(PS[:, 1, 2 * groups:3 * groups], ones[:], m[1], start=False, stop=True).then_inc(rank_ready, 1)

            def gather_half(s, b, turned, extra=None):
                for c in range(4):
                    for t in range(TT):
                        mm(PS[:, 6 + b, c * CAP:(c + 1) * CAP], h[:, t, (4 * b + c) * P:(4 * b + c + 1) * P],
                           pick[:, t, :], start=(t == 0), stop=(t == TT - 1))
                last = nc.tensor.transpose(PS[0:CAP, 6 + b, 4 * CAP:512], turned[:, b, :], ident[:])
                if extra:
                    last = extra()
                last.then_inc(s.gathered, 1)

            def scatter(s, i, per):
                for t in range(TT):
                    for hf in range(2):
                        if t:
                            pe.wait_ge(s.added, i * per + (hf + 2))
                        mm(bank(6 + hf), spread[0:CAP, t * P:(t + 1) * P], wk[4][0:CAP, hf * HALF:(hf + 1) * HALF],
                           start=True, stop=True).then_inc(s.scattered, 1)

            def three(o, left, right, first, last_one):
                (left_high, left_low), (right_high, right_low) = left, right
                mm(o, left_high, right_high, start=first, stop=False)
                mm(o, left_high, right_low, start=False, stop=False)
                return mm(o, left_low, right_high, start=False, stop=last_one)

            def moe_tile(s, i, k):
                kind, j, m = order[k]
                pe.wait_ge(s.low_taken, i * TILES1 + (k + 1))
                if kind == "d":
                    for c in range(2):
                        f = 2 * m + c
                        for hf in range(2):
                            a = slice(hf * HALF, (hf + 1) * HALF)
                            last = three(PS[0:CAP, 4 + hf, :], (hg_high[:, f, :], hg_low[:, f, :]),
                                         (split(w_high, k, 2)[:, c, a], split(w_low, k, 2)[:, c, a]),
                                         j == 0 and f == 0, k == TILES1 - 1 and c == 1)
                else:
                    n = 4 if ffn_chunks(j) == 4 else 8
                    o = PS[0:CAP, (0 if kind == "g" else 2) + j % 2, 0:TILE // n]
                    for c in range(n):
                        f = n * m + c
                        last = three(o, (xg_high[:, f, :], xg_low[:, f, :]),
                                     (split(w_high, k, n)[:, c, :], split(w_low, k, n)[:, c, :]),
                                     f == 0, f == KC - 1)
                last.then_inc(s.used, 1)

            def turn_hidden(s, i, j):
                pe.wait_ge(s.hid_ready, i * GROUPS + (j + 1))
                for c in range(ffn_chunks(j)):
                    last = nc.tensor.transpose(PS[:, 6 + j % 2, c * CAP:(c + 1) * CAP],
                                               wk[2 + j % 2][0:CAP, c * P:(c + 1) * P], ident[0:CAP, 0:CAP])
                last.then_inc(s.turned, 1)

            GATE0 = 2

            def experts(s, i, last):
                for k in range(GATE0, TILES1):
                    if order[k][0] == "d" and order[k][2] == 0:
                        j = order[k][1]
                        if j == GROUPS - 1:
                            turn_hidden(s, i, j)
                            if not last:
                                pe.wait_ge(s.picked, i * 2 + 4)
                                gather_half(s, 0, pickg)
                            pe.wait_ge(s.hg_low, i * GROUPS + GROUPS)
                            if not last:
                                gather_half(s, 1, pickg)
                        else:
                            pe.wait_ge(s.hg_low, i * GROUPS + (j + 1))
                    moe_tile(s, i, k)
                    if k in turn_at[:-1]:
                        j = turn_at.index(k)
                        if j == 0:
                            pe.wait_ge(s.added, i * 5 + 1)
                        turn_hidden(s, i, j)
                if not last:
                    pe.wait_ge(s.xg_low, i + 2)
                    for k in range(GATE0):
                        moe_tile(s, i + 1, k)
                pe.wait_ge(s.y_ready, i + 1)
                scatter(s, i, 5)

            def sweep1(st, s, n):
                pe.wait_ge(s.picked, 2)
                pe.wait_ge(s.added, 1)
                for b in range(2):
                    gather_half(s, b, pickg)
                pe.wait_ge(s.xg_low, 1)
                for k in range(GATE0):
                    moe_tile(s, 0, k)
                with pe.Fori(0, n - 1) as i:
                    experts(s, i, False)
                experts(s, n - 1, True)

            def experts2(st, s, i):
                def gates():
                    for t in range(TT):
                        last = mm(PS[0:CAP, 0, 4 * CAP:4 * CAP + 4], pick[:, t, :], now2[:, 2:6, t],
                                  start=(t == 0), stop=(t == TT - 1))
                    return last

                pe.wait_ge(s.picked, i * 2 + 2)
                pe.wait_ge(s.added, i * 4 + 1)
                gather_half(s, 0, pick)
                gather_half(s, 1, pick, gates)
                pe.wait_ge(s.xg_by_scalar, i + 1)
                pe.wait_ge(s.xg_by_vector, i + 1)

                def gate_up(q):
                    if q >= 2:
                        pe.wait_ge(s.hid_ready, i * 4 + (q - 1))
                    for m, kind in enumerate(("g", "u")):
                        tile = by8(st.arrived(pe, ("moe2", kind, q), i))
                        for c in range(2):
                            for k in range(KC):
                                last = mm(PS[:, q % 2, (2 * m + c) * CAP:(2 * m + c + 1) * CAP],
                                          tile[:, k, c * P:(c + 1) * P], xg[:, k, :],
                                          start=(k == 0), stop=(k == KC - 1))
                    last.then_inc(s.gu_ready, 1)

                def down(q):
                    pe.wait_ge(s.hid_ready, i * 4 + (q + 1))
                    if q >= 2:
                        pe.wait_ge(s.y_by_vector, i * 4 + (q - 1))
                    tile = by2(st.arrived(pe, ("moe2", "d", q), i))
                    for hf in range(2):
                        for c in range(2):
                            last = mm(PS[0:CAP, 2 + 2 * (q % 2) + hf, :], wk[2 + q % 2][:, c * CAP:(c + 1) * CAP],
                                      tile[:, c, hf * HALF:(hf + 1) * HALF], start=(c == 0), stop=(c == 1))
                    last.then_inc(s.down_done, 1)

                gate_up(0)
                for q in range(1, 4):
                    gate_up(q)
                    down(q - 1)
                down(3)
                pe.wait_ge(s.y_by_vector, i * 4 + 4)
                scatter(s, i, 4)

            def sweep2(st, s, n):
                with pe.Fori(0, n) as i:
                    experts2(st, s, i)

            def sweeps(sweep, main, rest_s, st_rest, n, k):
                sweep(stream, main, n)
                pe.wait_ge(over_ready, k)
                more = pe.value_load(over[0:1, k - 1:k], min_val=0, max_val=1)
                with pe.If(more == 1):
                    sweep(st_rest, rest_s, n * (PASSES - 1))
                with pe.Else():
                    pe.nop()
                pe.nop()

            pe.wait_ge(consts_made, 1)
            pe.wait_ge(rows_landed, 16 * 10)
            nc.tensor.transpose(PS[:, 0, 0:NROW], rows, ident[0:NROW, 0:NROW])
            for l in range(2):
                w = CH * TAPS
                last = nc.tensor.transpose(PS[:, 0, NROW + l * w:NROW + (l + 1) * w], rowsw[:, l, :], ident[0:w, 0:w])
            last.then_inc(params_turned, 1)
            pe.wait_ge(sgu_masked, 2)
            for l in range(2):
                for hd in range(4):
                    last = nc.tensor.transpose(PS[:, 2 + l, hd * P:(hd + 1) * P], wk[l][:, hd * P:(hd + 1) * P], ident[:])
            last.then_inc(params_turned, 1)
            pe.wait_ge(small_landed, 16 * 14)
            for k in range(2):
                for t in range(TT):
                    last = nc.tensor.transpose(PS[:, 4, k * S + t * P:k * S + (t + 1) * P],
                                               ptok[:, t, k * P:(k + 1) * P], ident[:])
            last.then_inc(params_turned, 1)
            pe.wait_ge(params_ready, 3)
            turn(0)
            mixer(0)
            turn(1)
            dense()
            turn(2)
            mixer(1)
            turn(3)
            route(3, router1, EXPERTS, EXPERTS, 1)
            sweeps(sweep1, main1, rest1, restream1, EXPERTS, 1)
            turn(5)
            have_hT(5)

            for t in range(TT):
                for c in range(KC):
                    last = mm(PS[:, 6, t * HEADS:(t + 1) * HEADS], hT[:, c, t * P:(t + 1) * P], wf[:, c, :],
                              start=(c == 0), stop=(c == KC - 1))
            last.then_inc(f_ready, 1)
            project_T(landed_pair("q"), 0).then_inc(proj2, 1)
            project_T(landed_pair("k"), 2).then_inc(proj2, 1)
            project(landed_pair("v"), 4).then_inc(proj2, 1)
            pe.wait_ge(log_step, LOG_F)
            mm(PS[:, 7, 0:8], upper[:], lf[:, 0, :], start=True, stop=True)
            mm(PS[:, 7, 8:16], ones[:], lf[:, 0, :], start=True, stop=False)
            mm(PS[:, 7, 8:16], upper[:], lf[:, 1, :], start=False, stop=True)
            mm(PS[0:HEADS, 7, 128:256], lf[:, 0, :], upper[:], start=True, stop=True)
            mm(PS[0:HEADS, 7, 256:384], lf[:, 0, :], ones[:], start=True, stop=False)
            mm(PS[0:HEADS, 7, 256:384], lf[:, 1, :], upper[:], start=False, stop=True).then_inc(cum_ready, 1)
            pe.wait_ge(cum_copied, 1)
            for w in range(2):
                pe.wait_ge(qk_sq, w + 1)
                if w:
                    pe.wait_ge(qk_std, 1)
                for b in range(2):
                    last = mm(bank(6 + b), block64[:], wk[w][:, b * HALF:(b + 1) * HALF], start=True, stop=True)
                last.then_inc(qk_ms, 1)
            for name, b, freed, value in (("cb", 0, qk_hat, 1), ("cc", 2, qk_hat, 2), ("cu", 4, v2_copied, 1),
                                          ("ga0", 0, cbu_copied, 1), ("ga1", 6, qk_std, 2), ("gb0", 4, cbu_copied, 2),
                                          ("gb1", 0, gates_act, 1)):
                pe.wait_ge(freed, value)
                project_T(landed_pair(name), b).then_inc(proj2, 1)
            pe.wait_ge(cc_used, 1)
            pe.wait_ge(gates_act, 4)
            for t in range(TT):
                n, each = P * (t + 1), 4 // (t + 1)
                for hd in range(HEADS):
                    o = PS[:, 2 + 2 * t + hd // each, (hd % each) * n:(hd % each + 1) * n]
                    mm(o, qz[:, hd, t * P:(t + 1) * P], uT[:, hd // 2, 0:n], start=True, stop=False)
                    last = mm(o, head_row[0:HEADS, hd, :], negc[:, 0:n], start=False, stop=True)
                last.then_inc(att_logits, 1)
            for t in range(TT):
                L, nk = (L1 if t else L0), t + 1
                pe.wait_ge(att_exp, HEADS * (t + 1))
                for b in range(2 * nk):
                    for c in range(4):
                        hd, kt = (4 * b + c) // nk, (4 * b + c) % nk
                        last = nc.tensor.transpose(PS[:, 2 + 2 * t + b, c * P:(c + 1) * P],
                                                   L[:, hd, kt * P:(kt + 1) * P], ident[:])
                    last.then_inc(att_turned, 1)
                pe.wait_ge(att_pT_s, (1, 3)[t])
                pe.wait_ge(att_pT_v, (1, 3)[t])
                for hd in range(HEADS):
                    for kt in range(nk):
                        last = mm(PS[:, 0, hd * 64:(hd + 1) * 64], PT[:, hd * nk + kt, :], vn[:, kt, hd * 64:(hd + 1) * 64],
                                  start=(kt == 0), stop=(kt == nk - 1))
                last.then_inc(att_out, 1)
                pe.wait_ge(att_y, t + 1)
                if t:
                    pe.wait_ge(att_yT, t)
                for c in range(4):
                    last = nc.tensor.transpose(PS[:, 1, c * P:(c + 1) * P], wk[2 + t][:, c * P:(c + 1) * P], ident[:])
                last.then_inc(att_yturned, 1)
            for k, (name, b, half) in enumerate((("out_att", 0, 0), ("out_conv2", 4, 4))):
                if k == 0:
                    pe.wait_ge(att_yT, 2)
                else:
                    pe.wait_ge(yconv, 1)
                pair = landed_pair(name)
                for c in range(KC):
                    for kk in range(4):
                        last = mm(chunks(b, 4)[:, c, :], by2(pair[kk // 2])[:, kk % 2, c * P:(c + 1) * P], yT[:, half + kk, :],
                                  start=(kk == 0), stop=(kk == 3))
                    if c % 4 == 3:
                        last.then_inc(merge_mm, 1)
            mT = sgu[:, 0:2, :].rearrange("p a (c s) -> p (a c) s", s=S)
            pe.wait_ge(merged, 2)
            rows_of_model("o", lambda k: mT[:, k, :], 0, True, True, o_done, 8)
            turn(6)
            route(6, router2, 20, GROUPS2, 2)
            sweeps(sweep2, main2, rest2, restream2, GROUPS2, 2)
            pe.wait_ge(x_updated, 14)
            rows_of_model("ple", lambda k: pT[:, k, :], 4, True, True, pw_done, 2)
            turn(7)
            have_hT(7)
            rows_of_model("pg", lambda k: hT[:, k, :], 0, True, True, pg_done, 8)

        @block.vector
        def _(v):
            own = Own(v, vstep)
            tt, ts, stt = nc.vector.tensor_tensor, nc.vector.tensor_scalar, nc.vector.scalar_tensor_tensor
            copy = nc.vector.tensor_copy
            asked = [0]

            def rsqrt(n):
                asked[0] += 1
                v.wait_ge(rstd_ready, asked[0])

            def updated():
                for t in range(TT):
                    nc.vector.memset(tick[:, t:t + 1], 0.0).then_inc(x_updated, 1)

            def norm(n, turned=True):
                if n == 0:
                    v.wait_ge(x_landed, 32)
                else:
                    v.wait_ge(x_updated, 2 * n)
                own.link(nc.vector.tensor_tensor_reduce(h[:, 1, :], x[:, 1, :], x[:, 1, :], 1.0, 0.0, ALU.mult,
                                                        ALU.add, ss[:, 1:2]))
                v.wait_ge(sumsq_ready, n + 1)
                ts(ms[:, 0:2], ss[:], 1.0 / D, EPS, ALU.mult, ALU.add).then_inc(ms_ready, 1)
                rsqrt(2)
                v.wait_ge(gain_landed, 16 * (n + 1))
                dst = h if turned else x
                for t in range(TT):
                    stt(out=dst[:, t, :], in0=x[:, t, :], scalar=rstd[:, t:t + 1], in1=gain[:],
                        op0=ALU.mult, op1=ALU.mult).then_inc(norm_applied, 1)
                if turned:
                    k = n if n < 4 else n - 1
                    for t in range(TT):
                        v.wait_ge(h_turned, 4 * k + 2 * t + 2)
                        copy(hT[:, 4:8, t * P:(t + 1) * P],
                             bank(2 * t + 1).rearrange("p (c s) -> p c s", c=4)).then_inc(hT_by_vector, 1)

            def add_rows(b, signal, base):
                for t in range(TT):
                    v.wait_ge(signal, base + t)
                    tt(x[:, t, :], x[:, t, :], bank(b + 2 * t, 2), ALU.add).then_inc(x_updated, 1)

            def mixer(l):
                flat_v = vn[:].rearrange("p t n -> p (t n)")
                by_head = flat_v.rearrange("p (a n) -> p a n", n=P)
                acc = wk[1].rearrange("p (c s) -> p c s", c=CH)
                v.wait_ge(proj_done, 4 * l + 2)
                v.wait_ge(gate_act, l + 1)
                own.link(tt(cpad[:, :, PAD:], chunks(2), wk[0].rearrange("p (c s) -> p c s", c=CH), ALU.mult))
                v.wait_ge(params_ready, 3)

                def tap(k):
                    for c in range(CH):
                        w = wcol[:, l, 4 * k + c:4 * k + c + 1]
                        if k == 0:
                            ins = ts(acc[:, c, :], cpad[:, c, 0:S], w, pcol[:, 4 * l + c:4 * l + c + 1],
                                     ALU.mult, ALU.add)
                        else:
                            own.settle(behind=CH - 1)
                            ins = stt(out=acc[:, c, :], in0=cpad[:, c, k:k + S], scalar=w, in1=acc[:, c, :],
                                      op0=ALU.mult, op1=ALU.add)
                        if k == TAPS - 1 and c == CH - 1:
                            ins.then_inc(conv_done, 1)
                        else:
                            own.mark(ins)

                for k in range(9):
                    tap(k)
                v.wait_ge(v_act, l + 1)
                v.wait_ge(small_landed, 16 * 14)
                own.link(nc.vector.tensor_reduce(s8[:], by_head, AX_X, ALU.add))
                own.link(ts(s8[:], s8[:], 1.0 / P, None, ALU.mult))
                tt(by_head, by_head, s8[:].unsqueeze(2).to_broadcast([P, 8, P]), ALU.subtract).then_inc(v_centred, 1)
                for k in range(9, 11):
                    tap(k)
                v.wait_ge(v_squared, l + 1)
                own.link(nc.vector.tensor_reduce(s8[:], wk[3].rearrange("p (a n) -> p a n", n=P), AX_X, ALU.add))
                ts(ms[:], s8[:], 1.0 / P, EPS, ALU.mult, ALU.add).then_inc(ms_ready, 1)
                for k in range(11, 12):
                    tap(k)
                rsqrt(8)
                own.link(tt(by_head, by_head, rstd[:].unsqueeze(2).to_broadcast([P, 8, P]), ALU.mult))
                own.link(tt(vn[:], vn[:], sng[:, l, :].unsqueeze(1).to_broadcast([P, TT, HALF]), ALU.mult))
                tt(vn[:], vn[:], snb[:, l, :].unsqueeze(1).to_broadcast([P, TT, HALF]), ALU.add).then_inc(v_ready, 1)
                for k in range(12, 15):
                    tap(k)
                v.wait_ge(mixed, l + 1)
                v.wait_ge(u_act, l + 1)
                m4 = PS[:, 4:6, :].rearrange("p b (h n t) -> p (b h) n t", n=TT, t=P)
                w4 = wk[0].rearrange("p (h n t) -> p h n t", h=4, n=TT)
                for n in range(TT):
                    own.link(tt(w4[:, :, n, :], m4[:, :, n, :], sgb[:, l], ALU.add))
                tt(yT[:, 4:8, :], uT[:], wk[0].rearrange("p (c s) -> p c s", c=CH), ALU.mult).then_inc(sgu_out, 1)
                for k in range(15, TAPS):
                    tap(k)
                v.wait_ge(conv_done, l + 1)
                v.wait_ge(mean_done, l + 1)
                tt(wk[1], wk[1], bank(0, 2), ALU.subtract).then_inc(centred, 1)
                v.wait_ge(std_done, l + 1)
                for hf in range(2):
                    a = slice(hf * HALF, (hf + 1) * HALF)
                    own.link(nc.vector.reciprocal(wk[2][:, a], wk[2][:, a]))
                    tt(wk[1][:, a], wk[1][:, a], wk[2][:, a], ALU.mult).then_inc(conv_hat, 1)
                add_rows(4, out_done, 8 * l + 7)

            def dense():
                for j in range(HALVES):
                    v.wait_ge(silu_ready, j + 1)
                    if j >= 2:
                        v.wait_ge(down_done, j - 1)
                    tt(wk[2 + j % 2][:, 0:512], wk[j % 2][:, 0:512], bank(2 + j % 2), ALU.mult).then_inc(hid_ready, 1)
                v.wait_ge(down_done, HALVES)
                for t in range(TT):
                    tt(x[:, t, :], x[:, t, :], bank(4 + 2 * t, 2), ALU.add).then_inc(x_updated, 1)

            def places(values, rows_, n, dst):
                shape = [P, rows_, n, n]
                gt = pair_gt[:, 0:rows_ * n * n].rearrange("p (r i j) -> p r i j", i=n, j=n)
                eq = pair_eq[:, 0:rows_ * n * n].rearrange("p (r i j) -> p r i j", i=n, j=n)
                other, self_ = values.unsqueeze(2).to_broadcast(shape), values.unsqueeze(3).to_broadcast(shape)
                own.mark(tt(gt, other, self_, ALU.is_gt))
                own.link(tt(eq, other, self_, ALU.is_equal))
                own.link(tt(eq, eq, tie[:, 0:n, 0:n].unsqueeze(1).to_broadcast(shape), ALU.mult))
                own.link(tt(gt, gt, eq, ALU.add))
                own.link(nc.vector.tensor_reduce(dst, gt, AX_X, ALU.add))

            def over_flag(k, groups):
                own.link(nc.vector.tensor_reduce(over_f[:, 0:1], PS[:, 1, 2 * groups:3 * groups], AX_X, ALU.max))
                own.link(ts(over_f[:, 1:2], over_f[:, 0:1], float(CAP), None, ALU.is_gt))
                copy(over[0:1, k - 1:k], over_f[0:1, 1:2]).then_inc(over_ready, 1)

            def route():
                v.wait_ge(logits_ready, 1)
                l8, m8 = lg[:, :, 0:EXPERTS], mk[:, :, 0:EXPERTS]
                own.link(copy(l8, PS[:, 0, 0:TT * EXPERTS].rearrange("p (t e) -> p t e", t=TT)))
                own.link(nc.vector.tensor_reduce(mx[:, 0:TT], l8, AX_X, ALU.max))
                tt(shifted[:, :, 0:EXPERTS], l8, mx[:, 0:TT].unsqueeze(2).to_broadcast([P, TT, EXPERTS]),
                   ALU.subtract).then_inc(exps_wanted, 1)
                places(l8, TT, EXPERTS, cnt[:, :, 0:EXPERTS])
                ts(m8, cnt[:, :, 0:EXPERTS], 1.5, None, ALU.is_lt).then_inc(mask_ready, 1)
                v.wait_ge(mask_ready, 1)
                v.wait_ge(exps_ready, 1)
                e8 = ex[:, :, 0:EXPERTS]
                own.link(tt(e8, e8, m8, ALU.mult))
                own.link(nc.vector.tensor_reduce(den[:, 0:TT], e8, AX_X, ALU.add))
                own.link(nc.vector.reciprocal(den[:, 0:TT], den[:, 0:TT]))
                own.link(tt(e8, e8, den[:, 0:TT].unsqueeze(2).to_broadcast([P, TT, EXPERTS]), ALU.mult))
                v.wait_ge(rank_ready, 1)
                rank = PS[:, 1, 0:TT * EXPERTS].rearrange("p (t e) -> p e t", t=TT)
                for p in range(PASSES):
                    c = slice(p * EXPERTS, (p + 1) * EXPERTS)
                    own.mark(ts(table[:, c, 0, :], rank, float(-p * CAP), None, ALU.add))
                    own.mark(copy(table[:, c, 1, :], m8.rearrange("p t e -> p e t")))
                    own.mark(copy(table[:, c, 2, :], e8.rearrange("p t e -> p e t")))
                over_flag(1, EXPERTS)

            def route2():
                v.wait_ge(logits_ready, 2)
                own.link(tt(lg[:], PS[:, 0, 0:TT * 20].rearrange("p (t e) -> p t e", t=TT),
                            bias2[:].unsqueeze(1).to_broadcast([P, TT, 20]), ALU.add))
                four = lambda a: a.rearrange("p t (g e) -> p t g e", e=4)
                own.link(nc.vector.tensor_reduce(den[:], four(lg[:]), AX_X, ALU.max))
                tt(four(shifted[:]), four(lg[:]),
                   den[:].rearrange("p (t g) -> p t g", t=TT).unsqueeze(3).to_broadcast([P, TT, 5, 4]),
                   ALU.subtract).then_inc(exps_wanted, 1)
                for g in range(5):
                    places(lg[:, :, 4 * g:4 * g + 4], TT, 4, cnt[:, :, 4 * g:4 * g + 4])
                own.link(ts(mk[:, :, 4:20], cnt[:, :, 4:20], 1.5, None, ALU.is_lt))
                ts(mk[:, :, 0:4], cnt[:, :, 0:4], 0.5, None, ALU.is_lt).then_inc(mask_ready, 1)
                v.wait_ge(mask_ready, 2)
                v.wait_ge(exps_ready, 2)
                own.link(tt(ex[:, :, 4:20], ex[:, :, 4:20], mk[:, :, 4:20], ALU.mult))
                own.link(nc.vector.tensor_reduce(den[:], four(ex[:]), AX_X, ALU.add))
                own.link(nc.vector.reciprocal(den[:], den[:]))
                d5 = den[:].rearrange("p (t g) -> p t g", t=TT)
                own.link(tt(four(ex[:]), four(ex[:]), d5.unsqueeze(3).to_broadcast([P, TT, 5, 4]), ALU.mult))
                for t in range(TT):
                    own.link(ts(ex[:, t, 4:20], ex[:, t, 4:20], d5[:, t, 0:1], None, ALU.mult))
                v.wait_ge(rank_ready, 2)
                rank = PS[:, 1, 0:TT * GROUPS2].rearrange("p (t e) -> p e t", t=TT)
                for p in range(PASSES):
                    c = slice(p * GROUPS2, (p + 1) * GROUPS2)
                    own.mark(ts(table2[:, c, 0, :], rank, float(-p * CAP), None, ALU.add))
                    own.mark(copy(table2[:, c, 1, :], mk[:, :, 0:4].rearrange("p t e -> p e t")))
                    for t in range(TT):
                        own.mark(copy(table2[:, c, 2:6, t], ex[:, t, 4:20].rearrange("p (g e) -> p g e", e=4)))
                over_flag(2, GROUPS2)

            def choose(s, i, fields, src, weighted):
                copy(fields[:], src).then_inc(s.picked, 1)
                v.wait_ge(s.picked, i * 2 + 1)
                for t in range(TT):
                    last = ts(pick[:, t, :], slot_no[:], fields[:, 0, t:t + 1], fields[:, 1, t:t + 1],
                              ALU.is_equal, ALU.mult)
                    if weighted:
                        last = ts(pickg[:, t, :], slot_no[:], fields[:, 0, t:t + 1], fields[:, 2, t:t + 1],
                                  ALU.is_equal, ALU.mult)
                last.then_inc(s.picked, 1)

            def at(tab, i):
                return tab[:, bass.ds(i, 1), :, :].rearrange("p a f t -> p (a f) t")

            def gathered(s, i):
                copy(xg[:, 4:8, :], bank(7)[:, 0:4 * CAP].rearrange("p (c s) -> p c s", c=4))
                copy(spread[0:CAP, P:S], PS[0:CAP, 7, 4 * CAP:512]).then_inc(s.xg_by_vector, 1)

            def add_scattered(s, i):
                for t in range(TT):
                    for hf in range(2):
                        v.wait_ge(s.scattered, i * 4 + (2 * t + hf + 1))
                        o = x[:, t, hf * HALF:(hf + 1) * HALF]
                        tt(o, o, bank(6 + hf), ALU.add).then_inc(s.added, 1)

            def low(st, s, i, k):
                v.wait_ge(s.high_taken, i * TILES1 + (k + 1))
                tt(w_low[:, k % SPLITS, :], slot(st.where[("moe", k)][0]), w_high[:, k % SPLITS, :].bitcast(F32),
                   ALU.subtract).then_inc(s.low_taken, 1)

            def hidden_rows(s, i, j):
                m = P * ffn_chunks(j)
                v.wait_ge(s.silu_ready, i * GROUPS + (j + 1))
                tt(wk[2 + j % 2][0:CAP, 0:m], wk[j % 2][0:CAP, 0:m], PS[0:CAP, 2 + j % 2, 0:m],
                   ALU.mult).then_inc(s.hid_ready, 1)

            def hidden_low(s, i, j):
                m = ffn_chunks(j)
                v.wait_ge(s.hg_high, i * GROUPS + (j + 1))
                tt(hg_low[:, 0:m, :], bank(6 + j % 2)[:, 0:m * CAP].rearrange("p (c s) -> p c s", c=m),
                   hg_high[:, 0:m, :].bitcast(F32), ALU.subtract).then_inc(s.hg_low, 1)

            def tokens_low(s, i, turned):
                for b in range(2):
                    v.wait_ge(s.xg_high, i * 2 + (b + 1))
                    copy(turned[0:CAP, b * P:(b + 1) * P], PS[0:CAP, 6 + b, 4 * CAP:512])
                    last = tt(xg_low[:, 4 * b:4 * b + 4, :], bank(6 + b)[:, 0:4 * CAP].rearrange("p (c s) -> p c s", c=4),
                              xg_high[:, 4 * b:4 * b + 4, :].bitcast(F32), ALU.subtract)
                last.then_inc(s.xg_low, 1)

            def experts(st, s, i, base, last):
                for k in range(SPLITS, TILES1 + SPLITS):
                    if k < TILES1:
                        low(st, s, i, k)
                    elif not last:
                        low(st, s, i + 1, k - TILES1)
                    for j in range(GROUPS):
                        if k == up_end[j] + SPLITS:
                            hidden_rows(s, i, j)
                        if k == turn_at[j] + SPLITS:
                            hidden_low(s, i, j)
                    if k == turn_at[-1] + SPLITS and not last:
                        tokens_low(s, i + 1, spread_next)
                if not last:
                    choose(s, i + 2, now, at(table, i + (base + 2)), True)
                add_scattered(s, i)
                if not last:
                    copy(spread[0:CAP, :], spread_next).then_inc(s.added, 1)

            def experts2(s, i, base):
                v.wait_ge(s.gathered, i * 2 + 2)
                copy(cws[0:CAP, :], PS[0:CAP, 0, 4 * CAP:4 * CAP + 4])
                gathered(s, i)
                choose(s, i + 1, now2, at(table2, i + (base + 1)), False)
                v.wait_ge(s.picked, i * 2 + 4)

                def hidden(q):
                    v.wait_ge(s.silu_ready, i * 4 + (q + 1))
                    if q >= 2:
                        v.wait_ge(s.down_done, i * 4 + (q - 1))
                    tt(wk[2 + q % 2][:, 0:2 * CAP], wk[q % 2][:, 0:2 * CAP], bank(q % 2)[:, 2 * CAP:4 * CAP],
                       ALU.mult).then_inc(s.hid_ready, 1)

                def weigh(q):
                    y = PS[0:CAP, 2 + 2 * (q % 2):4 + 2 * (q % 2), :].rearrange("p b n -> p (b n)")
                    v.wait_ge(s.down_done, i * 4 + (q + 1))
                    if q == 0:
                        ins = ts(wk[4][0:CAP, :], y, cws[0:CAP, 0:1], None, ALU.mult)
                    else:
                        v.wait_ge(s.y_by_vector, i * 4 + q)
                        ins = stt(out=wk[4][0:CAP, :], in0=y, scalar=cws[0:CAP, q:q + 1], in1=wk[4][0:CAP, :],
                                  op0=ALU.mult, op1=ALU.add)
                    ins.then_inc(s.y_by_vector, 1)

                hidden(0)
                hidden(1)
                weigh(0)
                hidden(2)
                weigh(1)
                hidden(3)
                weigh(2)
                weigh(3)
                add_scattered(s, i)

            def sweep1(st, s, base, n):
                nc.vector.memset(tick[:, 2:3], 0.0).then_inc(s.added, 1)
                choose(s, 0, now, table[:, base, :, :], True)
                for k in range(SPLITS):
                    low(st, s, 0, k)
                tokens_low(s, 0, spread)
                choose(s, 1, now, table[:, base + 1, :, :], True)
                with v.Fori(0, n - 1) as i:
                    experts(st, s, i, base, False)
                experts(st, s, n - 1, base, True)
                v.wait_ge(s.added, 5 * n)

            def sweep2(st, s, base, n):
                nc.vector.memset(tick[:, 2:3], 0.0).then_inc(s.added, 1)
                choose(s, 0, now2, table2[:, base, :, :], False)
                with v.Fori(0, n) as i:
                    experts2(s, i, base)
                v.wait_ge(s.added, 4 * n + 1)

            def sweeps(sweep, main, rest_s, st_rest, n, k):
                v.wait_ge(over_ready, k)
                sweep(stream, main, 0, n)
                more = v.value_load(over[0:1, k - 1:k], min_val=0, max_val=1)
                with v.If(more == 1):
                    sweep(st_rest, rest_s, n, n * (PASSES - 1))
                with v.Else():
                    v.nop()
                updated()

            norm(0)
            mixer(0)
            norm(1)
            dense()
            norm(2)
            mixer(1)
            norm(3)
            route()
            sweeps(sweep1, main1, rest1, restream1, EXPERTS, 1)
            norm(4, turned=False)
            v.wait_ge(norm_applied, 10)
            updated()
            norm(5)

            v.wait_ge(f_ready, 1)
            own.link(tt(lf[:], PS[:, 6, 0:16].rearrange("p (t e) -> p t e", t=TT),
                        bf[:].unsqueeze(1).to_broadcast([P, TT, HEADS]), ALU.add))
            own.link(ts(hs[:, 0:2, :], lf[:], -1.0, None, ALU.mult))
            tt(hs[:, 0:2, :], hs[:, 0:2, :], lf[:], ALU.max).then_inc(log_step, 1)
            v.wait_ge(h_turned, 20)
            for o in range(2):
                own.mark(nc.vector.memset(qz[64 * o:64 * o + 64, 1 - o::2, :], 0.0))
            v.wait_ge(log_step, LN_Z)
            stt(out=lf[:], in0=lf[:], scalar=0.0, in1=hs[:, 4:6, :], op0=ALU.min, op1=ALU.subtract).then_inc(log_step, 1)
            v.wait_ge(cum_ready, 1)
            own.mark(ts(c8[:].rearrange("p t e -> p (t e)"), PS[:, 7, 0:16], 8.0, None, ALU.mult))
            ts(negc, PS[0:HEADS, 7, 128:384], -8.0, None, ALU.mult).then_inc(cum_copied, 1)
            r = [wk[2 + w].rearrange("p (c s) -> p c s", c=CH) for w in range(2)]
            v.wait_ge(qk_std, 1)
            own.link(nc.vector.reciprocal(wk[2], wk[2]))
            for o in range(2):
                a = slice(64 * o, 64 * o + 64)
                last = stt(out=qz[a, o::2, :], in0=chunks(0)[a], scalar=pcol[a, 36:37], in1=r[0][a],
                           op0=ALU.mult, op1=ALU.mult)
            last.then_inc(qk_hat, 1)
            v.wait_ge(qk_std, 2)
            own.link(nc.vector.reciprocal(wk[3], wk[3]))
            stt(out=uT[:], in0=chunks(2), scalar=pcol[:, 37:38], in1=r[1], op0=ALU.mult,
                op1=ALU.mult).then_inc(qk_hat, 1)
            v.wait_ge(proj2, 5)
            v.wait_ge(cbu_copied, 2)
            cu = wk[1].rearrange("p (c s) -> p c s", c=CH)
            tt(cpad[:, :, PAD:], chunks(2), cu, ALU.mult).then_inc(cc_used, 1)
            v.wait_ge(cc_used, 1)
            off = PAD - (TAPS2 - 1)
            acc = wk[2].rearrange("p (c s) -> p c s", c=CH)
            for k in range(TAPS2):
                for c in range(CH):
                    w = pcol[:, 24 + 4 * k + c:25 + 4 * k + c]
                    if k == 0:
                        own.mark(ts(acc[:, c, :], cpad[:, c, off:off + S], w, None, ALU.mult))
                    else:
                        own.settle(behind=CH - 1)
                        own.mark(stt(out=acc[:, c, :], in0=cpad[:, c, off + k:off + k + S], scalar=w,
                                     in1=acc[:, c, :], op0=ALU.mult, op1=ALU.add))
            own.settle()
            v.wait_ge(cbu_copied, 1)
            tt(yT[:, 4:8, :], acc, wk[0].rearrange("p (c s) -> p c s", c=CH), ALU.mult).then_inc(yconv, 1)
            for t in range(TT):
                L, n, each = (L1 if t else L0), P * (t + 1), 4 // (t + 1)
                v.wait_ge(att_logits, t + 1)
                for hd in range(HEADS):
                    o = PS[:, 2 + 2 * t + hd // each, (hd % each) * n:(hd % each + 1) * n]
                    own.mark(stt(out=L[:, hd, :], in0=o, scalar=c8[:, t, hd:hd + 1], in1=causal[:, S - n:S],
                                 op0=ALU.add, op1=ALU.add))
                own.settle()
                own.link(nc.vector.tensor_reduce(negmax[:, t, :], L, AX_X, ALU.max))
                ts(negmax[:, t, :], negmax[:, t, :], -0.125, None, ALU.mult).then_inc(att_max, 1)
            for t in range(TT):
                for b in range(1, 2 * (t + 1), 2):
                    v.wait_ge(att_turned, 2 * t + b + 1)
                    copy(PT[:, 4 * b:4 * b + 4, :],
                         bank(2 + 2 * t + b).rearrange("p (c s) -> p c s", c=4)).then_inc(att_pT_v, 1)
                v.wait_ge(att_exp, HEADS * (t + 1))
                own.link(nc.vector.reciprocal(rowsum[:, t, :], rowsum[:, t, :]))
                v.wait_ge(att_out, t + 1)
                tt(wk[2 + t][:, 0:512].rearrange("p (h n) -> p h n", h=HEADS),
                   bank(0).rearrange("p (h n) -> p h n", h=HEADS),
                   rowsum[:, t, :].unsqueeze(2).to_broadcast([P, HEADS, 64]), ALU.mult).then_inc(att_y, 1)
            for k in range(2):
                v.wait_ge(merge_mm, k + 1)
                own.mark(tt(sgu[:, k, :], sgu[:, k, :], bank(2 * k, 2), ALU.mult))
            for k in range(2):
                v.wait_ge(merge_mm, 3 + k)
                own.link(tt(sgu[:, 2 + k, :], sgu[:, 2 + k, :], bank(4 + 2 * k, 2), ALU.mult))
                tt(sgu[:, k, :], sgu[:, k, :], sgu[:, 2 + k, :], ALU.add).then_inc(merged, 1)
            add_rows(0, o_done, 7)
            norm(6)
            route2()
            sweeps(sweep2, main2, rest2, restream2, GROUPS2, 2)
            norm(7)
            for t in range(TT):
                v.wait_ge(pw_done, t + 1)
                v.wait_ge(pg_act, t + 1)
                own.link(tt(wk[t], wk[t], bank(4 + 2 * t, 2), ALU.mult))
                tt(x[:, t, :], x[:, t, :], wk[t], ALU.add).then_inc(x_updated, 1)


def kernel(**inputs):
    import numpy as _np
    import concourse.bacc as _bacc
    from concourse import mybir as _mybir
    from concourse.bass_utils import run_bass_kernel_spmd as _run

    nc = _bacc.Bacc("TRN2", target_bir_lowering=False, num_devices=1)
    arrays, aps = {}, {}
    for name in INS:
        a = _np.ascontiguousarray(inputs[name])
        arrays[f"in_{name}_dram"] = a
        aps[name] = nc.dram_tensor(f"in_{name}_dram", a.shape, _mybir.dt.from_np(a.dtype), kind="ExternalInput").ap()
    out = nc.dram_tensor("out_dram", (1, S, D), _mybir.dt.float32, kind="ExternalOutput").ap()
    build(nc, aps, out)
    r = _run(nc, [arrays], core_ids=[0])
    return r.results[0]["out_dram"]
```
